# Optimizing a Trainium2 kernel written in Bass

```python
import math
import functools
import jax
import jax.numpy as jnp
from jax import lax
import numpy as np

D_MODEL = 1024
BATCH = 1
SEQ = 2048
DEPTH = 1
DEC_BATCH = 8
DEC_SEQ = 8
PAST_LEN = 8192
PAGE_SIZE = 128

N_HEADS = 4
HEAD_DIM = D_MODEL // 16
V_DIM = 2 * HEAD_DIM
ATTN_WIDTH = N_HEADS * V_DIM
QK_WIDTH = N_HEADS * 2 * HEAD_DIM
ATTN_SCALE = HEAD_DIM ** -0.5
CONV_CH = D_MODEL - ATTN_WIDTH
CONV_WIDTH = 31
IN_WIDTH = 2 * QK_WIDTH + ATTN_WIDTH + 2 * CONV_CH
N_EXPERTS = 64
N_GROUPS = 8
TOPK_GROUPS = 4
TOP_K = 8
D_EXPERT = D_MODEL // 4
D_SHARED = D_MODEL // 4
ROUTED_SCALE = 2.5
MOE_BLOCK = 64
Q_BLOCK = 128
DEEPNORM_ALPHA = (2 * DEPTH) ** 0.25
DEEPNORM_BETA = (8 * DEPTH) ** -0.25
NORM_EPS = 1e-5
NEG_INF = -1e30

kernel_name = "diffattn_conformer_moe_deepnorm_step"

def lambda_init(layer):
    return 0.8 - 0.6 * math.exp(-0.3 * layer)

def layer_norm(x, g, b):
    xf = x.astype(jnp.float32)
    mu = jnp.mean(xf, axis=-1, keepdims=True)
    var = jnp.mean(jnp.square(xf - mu), axis=-1, keepdims=True)
    y = (xf - mu) * lax.rsqrt(var + NORM_EPS)
    return (y * g.astype(jnp.float32) + b.astype(jnp.float32)).astype(x.dtype)

def rms_norm(x, g):
    xf = x.astype(jnp.float32)
    y = xf * lax.rsqrt(jnp.mean(jnp.square(xf), axis=-1, keepdims=True) + NORM_EPS)
    return (y * g.astype(jnp.float32)).astype(x.dtype)

def swiglu(x, w_gate, w_up, w_down):
    return (jax.nn.silu(x @ w_gate) * (x @ w_up)) @ w_down

def in_projection(x, w_in):
    b, s, _ = x.shape
    p = jnp.einsum("bsd,de->bse", x, w_in)
    q = p[..., :QK_WIDTH].reshape(b, s, N_HEADS, 2 * HEAD_DIM)
    k = p[..., QK_WIDTH:2 * QK_WIDTH].reshape(b, s, N_HEADS, 2 * HEAD_DIM)
    v = p[..., 2 * QK_WIDTH:2 * QK_WIDTH + ATTN_WIDTH].reshape(b, s, N_HEADS, V_DIM)
    glu_a, glu_b = jnp.split(p[..., 2 * QK_WIDTH + ATTN_WIDTH:], 2, axis=-1)
    return q, k, v, glu_a * jax.nn.sigmoid(glu_b)

def diff_lambda(lam_q1, lam_k1, lam_q2, lam_k2, lam_init):
    f = lambda a: a.astype(jnp.float32)
    return (jnp.exp(jnp.sum(f(lam_q1) * f(lam_k1)))
            - jnp.exp(jnp.sum(f(lam_q2) * f(lam_k2))) + lam_init)

def diff_attend(q, k, v, q_pos, k_pos, lam):
    causal = k_pos[None, :] <= q_pos[:, None]

    def attn_map(qh, kh):
        s = jnp.einsum("bqhd,bkhd->bhqk", qh, kh,
                       preferred_element_type=jnp.float32) * ATTN_SCALE
        return jax.nn.softmax(jnp.where(causal, s, NEG_INF), axis=-1)

    a = (attn_map(q[..., :HEAD_DIM], k[..., :HEAD_DIM])
         - lam * attn_map(q[..., HEAD_DIM:], k[..., HEAD_DIM:]))
    return jnp.einsum("bhqk,bkhe->bqhe", a, v.astype(jnp.float32)).astype(v.dtype)

def prompt_attention(q, k, v, lam):
    b, s = q.shape[:2]
    n_qb = s // Q_BLOCK
    q_blocks = q.reshape(b, n_qb, Q_BLOCK, N_HEADS, 2 * HEAD_DIM).swapaxes(0, 1)
    k_pos = jnp.arange(s)

    def block(args):
        i, q_blk = args
        return diff_attend(q_blk, k, v, i * Q_BLOCK + jnp.arange(Q_BLOCK), k_pos, lam)

    o = lax.map(block, (jnp.arange(n_qb), q_blocks))
    return o.swapaxes(0, 1).reshape(b, s, N_HEADS, V_DIM)

def sample_attention(q, k, v, lam, layer, cache_k, cache_v, page_table):
    ds = q.shape[1]
    past = page_table.shape[1] * cache_k.shape[2]
    q_pos = past + jnp.arange(ds)
    k_pos = jnp.arange(past + ds)

    def one_sequence(args):
        q_s, k_s, v_s, pages = args
        kk = jnp.concatenate(
            [cache_k[layer, pages].reshape(past, N_HEADS, 2 * HEAD_DIM), k_s], axis=0)
        vv = jnp.concatenate(
            [cache_v[layer, pages].reshape(past, N_HEADS, V_DIM), v_s], axis=0)
        return diff_attend(q_s[None], kk[None], vv[None], q_pos, k_pos, lam)[0]

    return lax.map(one_sequence, (q, k, v, page_table))

def conv_module(u, prev, w_dw, b_dw, ln_g, ln_b):
    ext = jnp.concatenate([prev.astype(u.dtype), u], axis=1)
    y = lax.conv_general_dilated(
        ext, w_dw[:, None, :].astype(u.dtype), window_strides=(1,), padding="VALID",
        dimension_numbers=("NWC", "WIO", "NWC"), feature_group_count=CONV_CH)
    y = jax.nn.silu(layer_norm(y + b_dw, ln_g, ln_b))
    return y, ext[:, -(CONV_WIDTH - 1):]

def routed_experts(t, idx, wts, w_gate, w_up, w_down):
    n, d = t.shape
    na = n * TOP_K
    flat_e = idx.reshape(-1)
    order = jnp.argsort(flat_e)
    sorted_e = flat_e[order]
    counts = jnp.bincount(flat_e, length=N_EXPERTS)
    padded = (counts + MOE_BLOCK - 1) // MOE_BLOCK * MOE_BLOCK
    start = jnp.cumsum(counts) - counts
    pstart = jnp.cumsum(padded) - padded
    rank = jnp.arange(na, dtype=jnp.int32) - start[sorted_e]
    dest = jnp.zeros((na,), jnp.int32).at[order].set((pstart[sorted_e] + rank).astype(jnp.int32))
    n_blocks = -(-na // MOE_BLOCK) + N_EXPERTS
    rows = n_blocks * MOE_BLOCK
    row_token = jnp.full((rows,), n, jnp.int32).at[dest].set(
        jnp.arange(na, dtype=jnp.int32) // TOP_K)
    row_w = jnp.zeros((rows,), jnp.float32).at[dest].set(wts.reshape(-1))
    t_pad = jnp.concatenate([t, jnp.zeros((1, d), t.dtype)], axis=0)
    xb = t_pad[row_token].reshape(n_blocks, MOE_BLOCK, d)
    block_e = jnp.minimum(
        jnp.searchsorted(jnp.cumsum(padded), jnp.arange(n_blocks) * MOE_BLOCK, side="right"),
        N_EXPERTS - 1)

    def run(args):
        xs, rw, e = args
        return swiglu(xs, w_gate[e], w_up[e], w_down[e]) * rw[:, None].astype(xs.dtype)

    yb = lax.map(run, (xb, row_w.reshape(n_blocks, MOE_BLOCK), block_e)).reshape(rows, d)
    return jax.ops.segment_sum(yb, row_token, num_segments=n + 1)[:n]

def moe_ffn(h, w_router, b_router, w_gate, w_up, w_down, w_sh_gate, w_sh_up, w_sh_down):
    shp = h.shape
    t = h.reshape(-1, shp[-1])
    n = t.shape[0]
    scores = jax.nn.sigmoid(
        jnp.einsum("td,de->te", t, w_router, preferred_element_type=jnp.float32))
    sel = scores + b_router.astype(jnp.float32)
    grp_score = lax.top_k(sel.reshape(n, N_GROUPS, N_EXPERTS // N_GROUPS), 2)[0].sum(-1)
    _, gidx = lax.top_k(grp_score, TOPK_GROUPS)
    gmask = jnp.any(gidx[..., None] == jnp.arange(N_GROUPS), axis=1)
    sel = jnp.where(jnp.repeat(gmask, N_EXPERTS // N_GROUPS, axis=-1), sel, NEG_INF)
    _, idx = lax.top_k(sel, TOP_K)
    wts = jnp.take_along_axis(scores, idx, axis=-1)
    wts = wts / jnp.sum(wts, axis=-1, keepdims=True) * ROUTED_SCALE
    routed = routed_experts(t, idx, wts, w_gate, w_up, w_down)
    shared = swiglu(t, w_sh_gate, w_sh_up, w_sh_down)
    return (routed + shared).reshape(shp)

def decoder_layer(x, conv_prev, attend, lam_init, w_in, lam_q1, lam_k1, lam_q2, lam_k2,
                  subln_g, w_dw, b_dw, conv_ln_g, conv_ln_b, w_o, ln1_g, ln1_b,
                  w_router, b_router, w_gate, w_up, w_down, w_sh_gate, w_sh_up,
                  w_sh_down, ln2_g, ln2_b):
    b, s, _ = x.shape
    q, k, v, u = in_projection(x, w_in)
    lam = diff_lambda(lam_q1, lam_k1, lam_q2, lam_k2, lam_init)
    o = rms_norm(attend(q, k, v, lam), subln_g) * (1.0 - lam_init)
    c, conv_state = conv_module(u, conv_prev, w_dw, b_dw, conv_ln_g, conv_ln_b)
    mix = jnp.concatenate([o.reshape(b, s, ATTN_WIDTH), c], axis=-1) @ w_o
    x = layer_norm(DEEPNORM_ALPHA * x + mix, ln1_g, ln1_b)
    ffn = moe_ffn(x, w_router, b_router, w_gate, w_up, w_down, w_sh_gate, w_sh_up, w_sh_down)
    x = layer_norm(DEEPNORM_ALPHA * x + ffn, ln2_g, ln2_b)
    return x, k, v, conv_state

def setup_inputs(seed: int = 0) -> dict:
    key = jax.random.key(seed)
    ks = jax.random.split(key, 32)
    f32 = jnp.float32
    n_pages = PAST_LEN // PAGE_SIZE
    n_used = DEC_BATCH * n_pages
    n_pool = n_used + max(1, n_used // 4)

    def nrm(k, shape, scale):
        return jax.random.normal(k, shape, f32) * scale

    page_table = jax.random.permutation(ks[5], n_pool)[:n_used].reshape(
        DEC_BATCH, n_pages).astype(jnp.int32)
    return {
        "x_prompt": nrm(ks[0], (BATCH, SEQ, D_MODEL), 1.0),
        "x_sample": nrm(ks[1], (DEC_BATCH, DEC_SEQ, D_MODEL), 1.0),
        "cache_k": nrm(ks[2], (DEPTH, n_pool, PAGE_SIZE, N_HEADS, 2 * HEAD_DIM), 1.0),
        "cache_v": nrm(ks[3], (DEPTH, n_pool, PAGE_SIZE, N_HEADS, V_DIM), 1.0),
        "state_conv": nrm(ks[4], (DEPTH, DEC_BATCH, CONV_WIDTH - 1, CONV_CH), 0.5),
        "page_table": page_table,
        "w_in": nrm(ks[6], (DEPTH, D_MODEL, IN_WIDTH), D_MODEL ** -0.5),
        "lam_q1": nrm(ks[7], (DEPTH, HEAD_DIM), 0.1),
        "lam_k1": nrm(ks[8], (DEPTH, HEAD_DIM), 0.1),
        "lam_q2": nrm(ks[9], (DEPTH, HEAD_DIM), 0.1),
        "lam_k2": nrm(ks[10], (DEPTH, HEAD_DIM), 0.1),
        "subln_g": 1.0 + nrm(ks[11], (DEPTH, V_DIM), 0.02),
        "w_dw": nrm(ks[12], (DEPTH, CONV_WIDTH, CONV_CH), CONV_WIDTH ** -0.5),
        "b_dw": nrm(ks[13], (DEPTH, CONV_CH), 0.02),
        "conv_ln_g": 1.0 + nrm(ks[14], (DEPTH, CONV_CH), 0.02),
        "conv_ln_b": nrm(ks[15], (DEPTH, CONV_CH), 0.02),
        "w_o": nrm(ks[16], (DEPTH, D_MODEL, D_MODEL), DEEPNORM_BETA * D_MODEL ** -0.5),
        "ln1_g": 1.0 + nrm(ks[17], (DEPTH, D_MODEL), 0.02),
        "ln1_b": nrm(ks[18], (DEPTH, D_MODEL), 0.02),
        "w_router": nrm(ks[19], (DEPTH, D_MODEL, N_EXPERTS), D_MODEL ** -0.5),
        "b_router": nrm(ks[20], (DEPTH, N_EXPERTS), 0.01),
        "w_gate": nrm(ks[21], (DEPTH, N_EXPERTS, D_MODEL, D_EXPERT), D_MODEL ** -0.5),
        "w_up": nrm(ks[22], (DEPTH, N_EXPERTS, D_MODEL, D_EXPERT), D_MODEL ** -0.5),
        "w_down": nrm(ks[23], (DEPTH, N_EXPERTS, D_EXPERT, D_MODEL), DEEPNORM_BETA * D_EXPERT ** -0.5),
        "w_sh_gate": nrm(ks[24], (DEPTH, D_MODEL, D_SHARED), D_MODEL ** -0.5),
        "w_sh_up": nrm(ks[25], (DEPTH, D_MODEL, D_SHARED), D_MODEL ** -0.5),
        "w_sh_down": nrm(ks[26], (DEPTH, D_SHARED, D_MODEL), DEEPNORM_BETA * D_SHARED ** -0.5),
        "ln2_g": 1.0 + nrm(ks[27], (DEPTH, D_MODEL), 0.02),
        "ln2_b": nrm(ks[28], (DEPTH, D_MODEL), 0.02),
    }

def reference(x_prompt, x_sample, cache_k, cache_v, state_conv, page_table, w_in,
              lam_q1, lam_k1, lam_q2, lam_k2, subln_g, w_dw, b_dw, conv_ln_g, conv_ln_b,
              w_o, ln1_g, ln1_b, w_router, b_router, w_gate, w_up, w_down, w_sh_gate,
              w_sh_up, w_sh_down, ln2_g, ln2_b):
    y_p, y_s = x_prompt, x_sample
    k_p, v_p, c_p, k_s, v_s, c_s = [], [], [], [], [], []
    for l in range(DEPTH):
        lp = (w_in[l], lam_q1[l], lam_k1[l], lam_q2[l], lam_k2[l], subln_g[l], w_dw[l],
              b_dw[l], conv_ln_g[l], conv_ln_b[l], w_o[l], ln1_g[l], ln1_b[l],
              w_router[l], b_router[l], w_gate[l], w_up[l], w_down[l], w_sh_gate[l],
              w_sh_up[l], w_sh_down[l], ln2_g[l], ln2_b[l])
        li = lambda_init(l)
        prev_p = jnp.zeros((y_p.shape[0], CONV_WIDTH - 1, CONV_CH), y_p.dtype)
        y_p, kl, vl, cl = decoder_layer(y_p, prev_p, prompt_attention, li, *lp)
        k_p.append(kl)
        v_p.append(vl)
        c_p.append(cl)
        attend_s = functools.partial(sample_attention, layer=l, cache_k=cache_k,
                                     cache_v=cache_v, page_table=page_table)
        y_s, kl, vl, cl = decoder_layer(y_s, state_conv[l], attend_s, li, *lp)
        k_s.append(kl)
        v_s.append(vl)
        c_s.append(cl)
    return (y_p, y_s, jnp.stack(k_p), jnp.stack(v_p), jnp.stack(c_p),
            jnp.stack(k_s), jnp.stack(v_s), jnp.stack(c_s))


_drawn_inputs = setup_inputs


def setup_inputs(seed=0):
    import zlib

    import numpy as np

    out = dict(_drawn_inputs(seed))
    spreads = {}
    factors = {'lam_q2': 2.688,
     'lam_k2': 5.128,
     'conv_ln_g': 2.754,
     'conv_ln_b': 2.679,
     'ln2_g': 9.619,
     'ln2_b': 8.474,
     'lam_k1': 3.093,
     'subln_g': 2.831}
    for name, (base, spread) in spreads.items():
        noise = np.random.default_rng([zlib.crc32(name.encode()), seed]).standard_normal(out[name].shape)
        drawn = base * np.exp(spread * noise) if base else spread * noise
        out[name] = jnp.asarray(drawn.astype(out[name].dtype))
    for name, factor in factors.items():
        out[name] = (out[name] * factor).astype(out[name].dtype)
    return out
```

```python
from contextlib import ExitStack

import concourse.bass as bass
import concourse.mybir as mybir

ALU = mybir.AluOpType
ACT = mybir.ActivationFunctionType
AX = mybir.AxisListType
F32 = mybir.dt.float32
BF16 = mybir.dt.bfloat16
I32 = mybir.dt.int32
U32 = mybir.dt.uint32
ds = bass.ds

P = 128
D = 1024
KT = D // P
SEQ = 2048
QT = SEQ // P
NSEQ = 8
NEW = 8
TOK = SEQ + NSEQ * NEW
TT = -(-TOK // P)
TP = TT * P
TAIL = TOK - QT * P
H = 4
HD = 64
C = 512
IN_W = 5 * C
CHUNKS = [(c * 512, 512) for c in range(SEQ // 512)] + [(SEQ, P)]
NEG = -1.0e30
LAMBDA_INIT = 0.2
TILE_ALPHA = 2.0 ** 0.25
EPS = 1e-5


def sems(nc, ctx, *names):
    return [ctx.enter_context(nc.semaphore(n)) for n in names]


def wait(eng, sem, count):
    if not isinstance(count, int) or count > 0:
        eng.wait_ge(sem, count)


def held(eng, sem, count, passed):
    wait(eng, sem, count)
    eng.sem_inc(passed, 1)


def loop(eng, n, body):
    body(0)
    if n > 1:
        with eng.Fori(1, n) as i:
            body(i)


def constants(nc, g):
    with ExitStack() as ctx:
        zeroed, = sems(nc, ctx, "const_zeroed")
        valid_made, = sems(nc, ctx, "valid_made")
        block = ctx.enter_context(nc.Block())

        @block.gpsimd
        def _(pool):
            nc.gpsimd.memset(g.ident[:], 0.0)
            nc.gpsimd.memset(g.ident_bf[:], 0.0)
            nc.gpsimd.memset(g.causal[:], 0.0).then_inc(zeroed, 1)
            nc.gpsimd.memset(g.valid[:], 1.0).then_inc(valid_made, 1)
            nc.gpsimd.iota(g.iota_e[:], pattern=[[1, 8]], base=0, channel_multiplier=0,
                           allow_small_or_imprecise_dtypes=True)
            pool.wait_ge(zeroed, 1)
            pool.wait_ge(valid_made, 1)
            nc.gpsimd.affine_select(out=g.valid[:, QT:TT], in_=g.valid[:, QT:TT], compare_op=ALU.is_ge, fill=0.0,
                                    base=TAIL - 1, pattern=[[0, 1]], channel_multiplier=-1)
            for m in (g.ident, g.ident_bf):
                nc.gpsimd.affine_select(out=m[:], in_=m[:], compare_op=ALU.not_equal, fill=1.0, base=0,
                                        pattern=[[-1, P]], channel_multiplier=1)
            nc.gpsimd.affine_select(out=g.causal[:], in_=g.causal[:], compare_op=ALU.is_ge, fill=NEG, base=0,
                                    pattern=[[-1, P]], channel_multiplier=1)


TAPS = 31
PAST = TAPS - 1
EXT = PAST + NEW
UW = PAST + SEQ + NSEQ * EXT


def in_projection(nc, g):
    with ExitStack() as ctx:
        sb = lambda n, s, dt=F32: ctx.enter_context(nc.sbuf_tensor(n, s, dt))
        xT = sb("xT", [P, KT, TP])
        xin = [sb(f"xin{u}", [P, D]) for u in range(2)]
        wcol = [sb(f"wcol{u}", [P, KT, P]) for u in range(2)]
        feat = [sb(f"feat{u}", [P, TP]) for u in range(2)]
        rows = [sb(f"rows{u}", [P, TT, P]) for u in range(2)]
        units = [sb(f"glu{i}", [P, UW]) for i in range(H)]
        gate = sb("glu_gate", [P, TP])
        conv = sb("conv_sum", [P, TP])
        fresh = sb("glu_fresh", [P, H, TAIL])
        state = feat[0][:, 0:2 * C].rearrange("p (g c) -> p g c", g=2)
        taps_in = rows[0][0:TAPS, 0:H, :]
        taps = sb("conv_taps", [P, H, TAPS])
        bias = sb("conv_bias", [P, H])
        last_p = rows[1][0:PAST, 0:H, :]
        last_s = rows[1][0:TAIL, H:2 * H, :]
        bank = [ctx.enter_context(nc.psum_tensor(f"p1_bank{b}", [P, 512], F32)) for b in range(8)]
        (small_in, state_turned, state_kept, zeroed, x_in0, x_in1, x_zeroed, xt_ready, xt_act, xt_dve, w_in0, w_in1,
         acc_ready, feat_ready, glu_ready, last_turned, last_kept, last_out, conv_step, conv_out, stored0,
         stored1, rows_ps, rows_ready, rows_out0, rows_out1, tail_out) = sems(
            nc, ctx, "small_in", "state_turned", "state_kept", "units_zeroed", "x_in0", "x_in1", "x_zeroed",
            "xt_ready", "xt_act", "xt_dve", "w_in0", "w_in1", "acc_ready", "feat_ready", "glu_ready", "last_turned",
            "last_kept", "last_out", "conv_step", "conv_out", "feat_stored0", "feat_stored1", "rows_ps",
            "rows_ready", "rows_out0", "rows_out1", "tail_out")
        x_in, w_arrived = (x_in0, x_in1), (w_in0, w_in1)
        feat_stored, rows_out = (stored0, stored1), (rows_out0, rows_out1)
        w_v = g.w_in.rearrange("(k p) n -> p k n", p=P)
        NCH = len(CHUNKS)
        QF, KF, VF = 2 * H, 3 * H, 4 * H
        sample = lambda i, a, b: units[i][:, PAST + SEQ:].rearrange("p (b r) -> p b r", r=EXT)[:, :, a:b]
        block = ctx.enter_context(nc.Block())

        @block.sync
        def _(sp):
            for half in range(2):
                sp.dma_start(state[0:4 * PAST, half, :], g.state_conv[0, 4 * half:4 * half + 4, :, :]
                             .rearrange("b r c -> (b r) c")).then_inc(small_in, 16)
            sp.dma_start(taps_in, g.w_dw[0].rearrange("j (i p) -> j i p", p=P)).then_inc(small_in, 16)
            with nc.allow_non_contiguous_dma("512 biases, one per channel"):
                sp.dma_start(bias[:], g.b_dw[0].rearrange("(i p) -> p i", p=P)).then_inc(small_in, 16)

            def load_x(i):
                for u in range(2):
                    wait(sp, xt_ready, (2 * i + u - 1) * 2)
                    sp.dma_start(xin[u][:], g.x_prompt[ds(i * 2 * P + u * P, P), :]).then_inc(x_in[u], 16)
            loop(sp, QT // 2, load_x)
            sp.wait_ge(x_zeroed, 1)
            sp.dma_start(xin[0][0:TAIL, :], g.x_sample).then_inc(x_in[0], 16)
            sp.wait_ge(x_in[0], 16 * (QT // 2 + 1))
            sp.dma_start(g.x_tail, xin[0][:]).then_inc(tail_out, 16)

            def load_w(first, column, i):
                for u in range(2):
                    wait(sp, acc_ready, (first + 2 * i + u - 1) * NCH)
                    sp.dma_start(wcol[u][:], w_v[:, :, ds(column(i, u), P)]).then_inc(w_arrived[u], 16)
            loop(sp, H, lambda i: load_w(0, lambda i, u: i * P + (4 * C - u * C), i))
            with sp.Fori(0, 3 * H // 2) as i:
                load_w(QF, lambda i, u: i * 2 * P + u * P, i)
            sp.wait_ge(tail_out, 16)

        @block.tensor
        def _(pe):
            pe.wait_ge(small_in, 64)
            for i in range(H):
                mm = nc.tensor.transpose(bank[4][:, i * 32:i * 32 + TAPS], taps_in[:, i, :], g.ident[0:TAPS, 0:TAPS])
            mm.then_inc(state_turned, 1)
            for half in range(2):
                for i in range(H):
                    mm = nc.tensor.transpose(bank[5 + half][:, i * P:i * P + 4 * PAST],
                                             state[0:4 * PAST, half, i * P:(i + 1) * P],
                                             g.ident[0:4 * PAST, 0:4 * PAST])
                mm.then_inc(state_turned, 1)

            def turn_x(u, tile, loaded):
                pe.wait_ge(x_in[u], loaded)
                for half, copied in ((0, xt_act), (1, xt_dve)):
                    wait(pe, copied, tile - 1)
                    for k in range(4):
                        mm = nc.tensor.transpose(bank[2 * u + half][:, k * P:(k + 1) * P],
                                                 xin[u][:, (4 * half + k) * P:(4 * half + k + 1) * P], g.ident[:])
                    mm.then_inc(xt_ready, 1)

            def turn_pair(i):
                for u in range(2):
                    turn_x(u, 2 * i + u, 16 * i + 16)
            loop(pe, QT // 2, turn_pair)
            turn_x(0, QT, 16 * (QT // 2 + 1))

            def products(u, c):
                s, n = CHUNKS[c]
                for k in range(KT):
                    mm = nc.tensor.matmul(bank[c][:, 0:n], wcol[u][:, k, :], xT[:, k, s:s + n],
                                          start=(k == 0), stop=(k == KT - 1))
                mm.then_inc(acc_ready, 1)

            def turn_rows(i, u, c):
                pe.wait_ge(feat_ready, (2 * i + (KF + u)) * NCH + (c + 1))
                wait(pe, rows_ready, (2 * i + u) * NCH + (c - 1))
                s, n = CHUNKS[c]
                for t in range(n // P):
                    mm = nc.tensor.transpose(bank[5 + (u * NCH + c) % 2][:, t * P:(t + 1) * P],
                                             feat[u][:, s + t * P:s + (t + 1) * P], g.ident[:])
                mm.then_inc(rows_ps, 1)

            def features(first, rows_too, i):
                for u in range(2):
                    pe.wait_ge(w_arrived[u], 16 * i + 16 * (first // 2 + 1))
                    for c in range(NCH):
                        wait(pe, feat_ready, (2 * i + (first + u - 1)) * NCH + (c + 1))
                        products(u, c)
                        if rows_too and c:
                            turn_rows(i, u, c - 1)
                    if rows_too:
                        turn_rows(i, u, NCH - 1)
            pe.wait_ge(xt_act, TT)
            pe.wait_ge(xt_dve, TT)
            pe.wait_ge(state_kept, 3)
            loop(pe, H, lambda i: features(0, False, i))
            with pe.Fori(0, H // 2) as i:
                features(QF, False, i)
            pe.wait_ge(glu_ready, H)
            for i in range(H):
                nc.tensor.transpose(bank[5][0:PAST, i * P:(i + 1) * P], units[i][:, SEQ:SEQ + PAST], g.ident[:])
                mm = nc.tensor.transpose(bank[6][0:TAIL, i * P:(i + 1) * P], fresh[:, i, :], g.ident[:])
            mm.then_inc(last_turned, 1)
            pe.wait_ge(last_kept, 2)
            loop(pe, H, lambda i: features(KF, True, i))

        @block.scalar
        def _(act):
            def keep_x(u, tile, column):
                act.wait_ge(xt_ready, 2 * tile + 1)
                nc.scalar.copy(xT[:, 0:4, ds(column, P)],
                               bank[2 * u][:].rearrange("p (k t) -> p k t", k=4)).then_inc(xt_act, 1)

            def keep_pair(i):
                for u in range(2):
                    keep_x(u, 2 * i + u, i * (2 * P) + u * P)
            loop(act, QT // 2, keep_pair)
            keep_x(0, QT, SEQ)

            for i in range(H):
                if i:
                    act.wait_ge(glu_ready, i)
                for c, (s, n) in enumerate(CHUNKS):
                    act.wait_ge(acc_ready, 2 * i * NCH + c + 1)
                    nc.scalar.activation(gate[:, s:s + n], bank[c][:, 0:n], ACT.Sigmoid).then_inc(feat_ready, 1)
                for c, (s, n) in enumerate(CHUNKS):
                    act.wait_ge(acc_ready, (2 * i + 1) * NCH + c + 1)
                    if s < SEQ:
                        nc.scalar.copy(units[i][:, PAST + s:PAST + s + n], bank[c][:, 0:n]).then_inc(feat_ready, 1)
                    else:
                        nc.scalar.copy(sample(i, PAST, EXT), bank[c][:, 0:TAIL].rearrange("p (b r) -> p b r", r=NEW)
                                       ).then_inc(feat_ready, 1)

            def keep_rows(i, u, c):
                act.wait_ge(rows_ps, (2 * i + u) * NCH + (c + 1))
                s, n = CHUNKS[c]
                nc.scalar.copy(rows[u][:, s // P:(s + n) // P, :],
                               bank[5 + (u * NCH + c) % 2][:, 0:n].rearrange("p (t f) -> p t f", f=P)
                               ).then_inc(rows_ready, 1)

            def keep_features(i, first, stored, kv):
                for u in range(2):
                    wait(act, feat_stored[u], stored)
                    if kv is not None:
                        wait(act, rows_ps, (kv + u - 1) * NCH)
                        wait(act, rows_out[u], 16 * kv)
                    for c, (s, n) in enumerate(CHUNKS):
                        act.wait_ge(acc_ready, (2 * i + (first + u)) * NCH + (c + 1))
                        nc.scalar.copy(feat[u][:, s:s + n], bank[c][:, 0:n]).then_inc(feat_ready, 1)
                        if kv is not None and c:
                            keep_rows(kv // 2, u, c - 1)
                    if kv is not None:
                        keep_rows(kv // 2, u, NCH - 1)
            act.wait_ge(state_turned, 3)
            loop(act, H // 2, lambda i: keep_features(i, QF, 16 * i, None))
            act.wait_ge(last_turned, 1)
            nc.scalar.copy(last_p, bank[5][0:PAST, :].rearrange("p (i c) -> p i c", c=P)).then_inc(last_kept, 1)
            nc.scalar.copy(last_s, bank[6][0:TAIL, :].rearrange("p (i c) -> p i c", c=P)).then_inc(last_kept, 1)
            act.wait_ge(last_out, 16 * (NSEQ + 2))
            keep_features(0, KF, 16 * (H // 2), 0)
            keep_features(1, KF, 16 * (H // 2 + 1), 2)
            keep_features(0, VF, 16 * H, H)
            keep_features(1, VF, 16 * H, H + 2)

        @block.vector
        def _(dve):
            for i in range(H):
                nc.vector.memset(units[i][:, 0:PAST], 0.0).then_inc(zeroed, 1)
            nc.vector.memset(conv[:, TOK:TP], 0.0).then_inc(zeroed, 1)
            dve.wait_ge(state_turned, 1)
            nc.vector.tensor_copy(taps[:], bank[4][:, 0:32 * H].rearrange("p (i j) -> p i j", j=32)[:, :, 0:TAPS]
                                  ).then_inc(state_kept, 1)
            for half in range(2):
                dve.wait_ge(state_turned, 2 + half)
                for i in range(H):
                    ins = nc.vector.tensor_copy(
                        sample(i, 0, PAST)[:, 4 * half:4 * half + 4, :],
                        bank[5 + half][:, i * P:i * P + 4 * PAST].rearrange("p (b r) -> p b r", r=PAST))
                ins.then_inc(state_kept, 1)

            def keep_x(u, tile, column):
                dve.wait_ge(xt_ready, 2 * tile + 2)
                nc.vector.tensor_copy(xT[:, 4:8, ds(column, P)],
                                      bank[2 * u + 1][:].rearrange("p (k t) -> p k t", k=4)).then_inc(xt_dve, 1)

            def keep_pair(i):
                for u in range(2):
                    keep_x(u, 2 * i + u, i * (2 * P) + u * P)
            loop(dve, QT // 2, keep_pair)
            dve.wait_ge(xt_ready, 2 * (QT - 1))
            nc.vector.memset(xin[0][:], 0.0).then_inc(x_zeroed, 1)
            keep_x(0, QT, SEQ)

            dve.wait_ge(zeroed, H + 1)
            dve.wait_ge(state_kept, 3)
            step = 0
            for i in range(H):
                dve.wait_ge(glu_ready, i + 1)
                if i:
                    dve.wait_ge(conv_out, 16 * i)
                for j in range(TAPS):
                    for what in range(2):
                        if j:
                            dve.wait_ge(conv_step, step - 1)
                        if what == 0:
                            src, acc = units[i][:, j:j + SEQ], conv[:, 0:SEQ]
                        else:
                            src = sample(i, j, j + NEW)
                            acc = conv[:, SEQ:TOK].rearrange("p (b r) -> p b r", r=NEW)
                        if j == 0:
                            nc.vector.tensor_scalar(acc, src, taps[:, i, 0:1], bias[:, i:i + 1], ALU.mult, ALU.add
                                                    ).then_inc(conv_step, 1)
                        else:
                            nc.vector.scalar_tensor_tensor(out=acc, in0=src, scalar=taps[:, i, j:j + 1], in1=acc,
                                                           op0=ALU.mult, op1=ALU.add).then_inc(conv_step, 1)
                        step += 1

        @block.gpsimd
        def _(pool):
            pool.dma_start(g.conv_sample[:, 0:PAST - NEW, :], g.state_conv[0, :, NEW:PAST, :]).then_inc(last_out, 16)
            for i in range(H):
                pool.wait_ge(feat_ready, 2 * (i + 1) * NCH)
                u = units[i][:, PAST:PAST + SEQ]
                nc.gpsimd.tensor_tensor(u, u, gate[:, 0:SEQ], ALU.mult)
                nc.gpsimd.tensor_tensor(fresh[:, i, :].rearrange("p (b r) -> p b r", r=NEW), sample(i, PAST, EXT),
                                        gate[:, SEQ:TOK].rearrange("p (b r) -> p b r", r=NEW), ALU.mult)
                nc.gpsimd.tensor_tensor(sample(i, PAST, EXT), sample(i, PAST, EXT),
                                        gate[:, SEQ:TOK].rearrange("p (b r) -> p b r", r=NEW), ALU.mult
                                        ).then_inc(glu_ready, 1)
            CONV_STEPS = 2 * TAPS

            def store_conv(i):
                pool.wait_ge(conv_step, CONV_STEPS * (i + 1))
                pool.dma_start(g.convT[i], conv[:]).then_inc(conv_out, 16)

            def store_feature(i, first, to):
                for u in range(2):
                    pool.wait_ge(feat_ready, (2 * i + first + u + 1) * NCH)
                    pool.dma_start(to[2 * i + u], feat[u][:]).then_inc(feat_stored[u], 16)

            def store_rows(i, at, to_prompt, to_sample):
                for u in range(2):
                    pool.wait_ge(rows_ready, (2 * i + at + u + 1) * NCH)
                    h = (2 * i + u) * P
                    pool.dma_start(to_prompt.rearrange("(t p) f -> p t f", p=P)[:, :, h:h + P],
                                   rows[u][:, 0:QT, :]).then_inc(rows_out[u], 16)
                    pool.dma_start(to_sample[:, h:h + P], rows[u][0:TAIL, QT, :]).then_inc(rows_out[u], 16)

            store_feature(0, QF, g.qT)
            store_feature(1, QF, g.qT)
            pool.wait_ge(last_kept, 2)
            pool.dma_start(g.conv_prompt, last_p.rearrange("p i c -> p (i c)")).then_inc(last_out, 16)
            for b in range(NSEQ):
                pool.dma_start(g.conv_sample[b, PAST - NEW:PAST, :], last_s[NEW * b:NEW * (b + 1)]
                               .rearrange("p i c -> p (i c)")).then_inc(last_out, 16)
            store_conv(0)
            store_feature(0, KF, g.kT)
            store_rows(0, 0, g.k_prompt, g.k_sample)
            store_conv(1)
            store_feature(1, KF, g.kT)
            store_rows(1, 0, g.k_prompt, g.k_sample)
            store_conv(2)
            store_rows(0, H, g.v_prompt, g.v_sample)
            store_conv(3)
            store_rows(1, H, g.v_prompt, g.v_sample)
            pool.wait_ge(last_out, 16 * (NSEQ + 2))
            pool.wait_ge(conv_out, 16 * H)
            for u in range(2):
                pool.wait_ge(feat_stored[u], 16 * H)
                pool.wait_ge(rows_out[u], 32 * H)


SCALE = float(HD) ** -0.5


def mixing_weight(nc, g):
    with ExitStack() as ctx:
        vec = ctx.enter_context(nc.sbuf_tensor("lam_vectors", [P, 4, HD], F32))
        prod = ctx.enter_context(nc.sbuf_tensor("lam_products", [P, 2, HD], F32))
        dot = ctx.enter_context(nc.sbuf_tensor("lam_dots", [P, 2], F32))
        ex = ctx.enter_context(nc.sbuf_tensor("lam_exps", [P, 2], F32))
        vectors_in, dot_done, exp_done, made = sems(nc, ctx, "lam_in", "lam_dot", "lam_exp", "lam_made")
        block = ctx.enter_context(nc.Block())

        @block.sync
        def _(sp):
            for n, v in enumerate((g.lam_q1, g.lam_k1, g.lam_q2, g.lam_k2)):
                sp.dma_start(vec[:, n, :], v.partition_broadcast(P)).then_inc(vectors_in, 16)

        @block.vector
        def _(dve):
            dve.wait_ge(vectors_in, 64)
            for n in range(2):
                nc.vector.tensor_tensor_reduce(prod[:, n, :], vec[:, 2 * n, :], vec[:, 2 * n + 1, :], 1.0, 0.0,
                                               ALU.mult, ALU.add, dot[:, n:n + 1]).then_inc(dot_done, 1)
            dve.wait_ge(exp_done, 1)
            nc.vector.tensor_scalar(ex[:, 1:2], ex[:, 1:2], -LAMBDA_INIT, None, ALU.add).then_inc(made, 1)
            dve.wait_ge(made, 1)
            nc.vector.tensor_tensor(g.neg_lam[:], ex[:, 1:2], ex[:, 0:1], ALU.subtract).then_inc(made, 1)

        @block.scalar
        def _(act):
            act.wait_ge(dot_done, 2)
            nc.scalar.activation(ex[:], dot[:], ACT.Exp).then_inc(exp_done, 1)


def prompt_attention(nc, g):
    with ExitStack() as ctx:
        sb = lambda n, s, dt=F32: ctx.enter_context(nc.sbuf_tensor(n, s, dt))
        q = [sb(f"q_head{u}", [P, SEQ]) for u in range(2)]
        k = [sb(f"k_head{u}", [P, SEQ]) for u in range(2)]
        v = [sb(f"v_head{u}", [P, QT, P]) for u in range(2)]
        out = [sb(f"o_head{u}", [P, QT, P]) for u in range(2)]
        prob = [[sb(f"prob{m}_{b}", [P, SEQ]) for m in range(2)] for b in range(2)]
        turned = [sb(f"mix_turned{b}", [P, 512]) for b in range(2)]
        mx = sb("row_max_parts", [P, 2, 2, 4])
        top = sb("row_max", [P, 2, 2])
        bias = sb("exp_bias", [P, 2, 2])
        part = sb("row_sum_parts", [P, 2, 2, 4])
        total = sb("row_sums", [P, 2, 2])
        recip = sb("row_recips", [P, 2, 2])
        coef = sb("mix_coef", [P, 2])
        ring = [ctx.enter_context(nc.psum_tensor(f"scores{b}", [P, 512], F32)) for b in range(5)]
        turn = [ctx.enter_context(nc.psum_tensor(f"turn{b}", [P, 512], F32)) for b in range(2)]
        o_ps = ctx.enter_context(nc.psum_tensor("o_ps", [P, 512], F32))
        (in0, in1, scores_ready, part_max, row_max, bias_ready, exp_done, summed, inverted, coef_ready, mixed, ps_turned,
         sb_turned, pv_done, o_kept, out_free, out0, out1) = sems(
            nc, ctx, "head_in0", "head_in1", "scores_ready", "part_max", "row_max", "bias_ready", "exp_done", "summed",
            "inverted", "coef_ready", "mixed", "ps_turned", "sb_turned", "pv_done", "o_kept", "out_free",
            "out_stored0", "out_stored1")
        head_in, stored = (in0, in1), (out0, out1)
        NCH = [qi // 4 + 1 for qi in range(QT)]
        before = [sum(NCH[:qi]) for qi in range(QT + 1)]
        GH, SH = before[QT], 2 * before[QT]
        RING, TURNS = len(ring), len(turn)
        width = lambda qi, c: min(512, (qi + 1) * P - c * 512)
        chunk_no = lambda qi, m, c: 2 * before[qi] + m * NCH[qi] + c
        E_FREE = NCH[QT - 1] + 1

        def steps(head):
            yield "scores", 0, 0
            yield "scores", 0, 1
            for qi in range(QT):
                if qi + 1 < QT:
                    yield "scores", qi + 1, 0
                yield "mix", qi, None
                if qi + 1 < QT:
                    yield "scores", qi + 1, 1

        block = ctx.enter_context(nc.Block())

        @block.sync
        def _(sp):
            def load(h):
                u = h % 2
                if h >= 2:
                    sp.wait_ge(pv_done, (h - 1) * GH + TURNS)
                sp.dma_start(q[u][:], g.qT[h, :, 0:SEQ]).then_inc(head_in[u], 16)
                sp.dma_start(k[u][:], g.kT[h, :, 0:SEQ]).then_inc(head_in[u], 16)
                sp.dma_start(v[u][:], g.v_prompt.rearrange("(t p) f -> p t f", p=P)[:, :, h * P:(h + 1) * P]
                             ).then_inc(head_in[u], 16)
            load(0)
            load(1)
            for h in range(H):
                u = h % 2
                sp.wait_ge(o_kept, (h + 1) * QT + 1)
                sp.dma_start(g.attn[0:SEQ, h * P:(h + 1) * P].rearrange("(t p) f -> p t f", p=P), out[u][:]
                             ).then_inc(stored[u], 16)
                if h + 2 < H:
                    load(h + 2)
                sp.wait_ge(stored[u], 16 * (h // 2 + 1))
                sp.sem_inc(out_free, 1)

        @block.tensor
        def _(pe):
            pe.sem_inc(ps_turned, E_FREE)
            pe.sem_inc(pv_done, TURNS)
            with pe.Fori(0, H // 2) as i:
                for u in range(2):
                    pe.wait_ge(head_in[u], 48 * i + 48)
                    for what, qi, m in steps(u):
                        if what == "scores":
                            for c in range(NCH[qi]):
                                n = chunk_no(qi, m, c)
                                b = ring[(u * SH + n) % RING]
                                pe.wait_ge(exp_done, i * (2 * SH) + (u * SH + n + 1))
                                w = width(qi, c)
                                last = c == NCH[qi] - 1
                                mm = nc.tensor.matmul(b[:, 0:w], q[u][m * HD:(m + 1) * HD, qi * P:(qi + 1) * P],
                                                      k[u][m * HD:(m + 1) * HD, c * 512:c * 512 + w],
                                                      start=True, stop=not last)
                                if last:
                                    mm = nc.tensor.matmul(b[:, w - P:w], g.ident_bf[:], g.causal[:],
                                                          start=False, stop=True)
                                mm.then_inc(scores_ready, 1)
                        else:
                            pe.wait_ge(mixed, i * (2 * QT) + (u * QT + qi + 1))
                            for c in range(NCH[qi] + 1):
                                if c < NCH[qi]:
                                    n = u * GH + before[qi] + c
                                    pe.wait_ge(sb_turned, i * (2 * GH) + (n + 1))
                                    for t in range(width(qi, c) // P):
                                        mm = nc.tensor.transpose(
                                            turn[n % TURNS][:, t * P:(t + 1) * P],
                                            prob[qi % 2][0][:, c * 512 + t * P:c * 512 + (t + 1) * P], g.ident[:])
                                    mm.then_inc(ps_turned, 1)
                                if c == 0:
                                    pe.wait_ge(o_kept, i * (2 * QT) + (u * QT + qi + 1))
                                    continue
                                n = u * GH + before[qi] + c - 1
                                pe.wait_ge(sb_turned, i * (2 * GH) + (n + 1 + TURNS))
                                for t in range(width(qi, c - 1) // P):
                                    key = 4 * (c - 1) + t
                                    mm = nc.tensor.matmul(o_ps[:, 0:P], turned[n % TURNS][:, t * P:(t + 1) * P],
                                                          v[u][:, key, :], start=(key == 0), stop=(key == qi))
                                mm.then_inc(pv_done, 1)

        @block.vector
        def _(dve):
            with dve.Fori(0, H // 2) as i:
                for u in range(2):
                    for what, qi, m in steps(u):
                        b = qi % 2
                        if what == "scores":
                            for c in range(NCH[qi]):
                                n = u * SH + chunk_no(qi, m, c)
                                dve.wait_ge(scores_ready, i * (2 * SH) + (n + 1))
                                nc.vector.tensor_reduce(mx[:, b, m, c:c + 1], ring[n % RING][:, 0:width(qi, c)],
                                                        AX.X, ALU.max).then_inc(part_max, 1)
                            dve.wait_ge(part_max, i * (2 * SH) + (n + 1))
                            nc.vector.tensor_reduce(top[:, b, m:m + 1], mx[:, b, m, 0:NCH[qi]], AX.X, ALU.max
                                                    ).then_inc(row_max, 1)
                            r = u * 2 * QT + 2 * qi + m + 1
                            dve.wait_ge(row_max, i * (4 * QT) + r)
                            nc.vector.tensor_scalar(bias[:, b, m:m + 1], top[:, b, m:m + 1], -SCALE, None, ALU.mult
                                                    ).then_inc(bias_ready, 1)
                        else:
                            r = u * QT + qi + 1
                            dve.wait_ge(exp_done, i * (2 * SH) + (RING + u * SH + 2 * before[qi + 1]))
                            nc.vector.tensor_reduce(total[:, b, :], part[:, b, :, 0:NCH[qi]], AX.X, ALU.add
                                                    ).then_inc(summed, 1)
                            dve.wait_ge(summed, i * (2 * QT) + r)
                            nc.vector.reciprocal(recip[:, b, :], total[:, b, :]).then_inc(inverted, 1)
                            dve.wait_ge(inverted, i * (2 * QT) + r)
                            nc.vector.scalar_tensor_tensor(out=coef[:, b:b + 1], in0=recip[:, b, 1:2],
                                                           scalar=total[:, b, 0:1], in1=g.neg_lam[:], op0=ALU.mult,
                                                           op1=ALU.mult).then_inc(coef_ready, 1)
                            dve.wait_ge(coef_ready, i * (2 * QT) + r)
                            w = (qi + 1) * P
                            nc.vector.scalar_tensor_tensor(out=prob[b][0][:, 0:w], in0=prob[b][1][:, 0:w],
                                                           scalar=coef[:, b:b + 1], in1=prob[b][0][:, 0:w],
                                                           op0=ALU.mult, op1=ALU.add).then_inc(mixed, 1)

        @block.scalar
        def _(act):
            act.sem_inc(exp_done, RING)
            act.sem_inc(sb_turned, TURNS)
            act.sem_inc(o_kept, 1)
            act.sem_inc(out_free, 2)
            with act.Fori(0, H // 2) as i:
                for u in range(2):
                    act.wait_ge(out_free, i * 2 + (u + 1))
                    for what, qi, m in steps(u):
                        b = qi % 2
                        if what == "scores":
                            act.wait_ge(bias_ready, i * (4 * QT) + (u * 2 * QT + 2 * qi + m + 1))
                            if m == 0:
                                last = before[qi - 1] if qi else -NCH[QT - 1]
                                act.wait_ge(ps_turned, i * (2 * GH) + (E_FREE + u * GH + last))
                            for c in range(NCH[qi]):
                                n = u * SH + chunk_no(qi, m, c)
                                w = width(qi, c)
                                nc.scalar.activation(prob[b][m][:, c * 512:c * 512 + w], ring[n % RING][:, 0:w],
                                                     ACT.Exp, bias=bias[:, b, m:m + 1], scale=SCALE,
                                                     accum_out=part[:, b, m, c:c + 1]).then_inc(exp_done, 1)
                        else:
                            for c in range(NCH[qi]):
                                n = u * GH + before[qi] + c
                                w = width(qi, c)
                                act.wait_ge(ps_turned, i * (2 * GH) + (n + 1 + E_FREE))
                                act.wait_ge(pv_done, i * (2 * GH) + (n + 1))
                                nc.scalar.copy(turned[n % TURNS][:, 0:w], turn[n % TURNS][:, 0:w]
                                               ).then_inc(sb_turned, 1)
                            act.wait_ge(pv_done, i * (2 * GH) + (u * GH + before[qi + 1] + TURNS))
                            nc.scalar.activation(out[u][:, qi, :], o_ps[:, 0:P], ACT.Copy,
                                                 scale=recip[:, b, 0:1]).then_inc(o_kept, 1)


PAGES = 64
ROUND = 16
ROUNDS = PAGES // ROUND
LOT = 4
LOTS = ROUND // LOT
LANES = P // LOT
COLS = H * 2 * NEW


def decode_attention(nc, g):
    with ExitStack() as ctx:
        sb = lambda n, s, dt=F32: ctx.enter_context(nc.sbuf_tensor(n, s, dt))
        table = sb("page_rows", [P, NSEQ * PAGES], I32)
        lane = sb("lane", [P, 1])
        row = sb("cache_rows", [P, NSEQ * PAGES // LOT], U32)
        klot = [sb(f"k_lot{x}", [P, LOT, C]) for x in range(LOTS)]
        vlot = [sb(f"v_lot{x}", [P, LOT, C]) for x in range(LOTS)]
        kpage = [klot[p // LOT][:, p % LOT, :] for p in range(ROUND)]
        vpage = [vlot[p // LOT][:, p % LOT, :] for p in range(ROUND)]
        kt = [sb(f"k_turned{n}", [P, C]) for n in range(4)]
        qz = sb("q_by_map", [P, NSEQ, H, 2 * NEW])
        knew = sb("k_new", [P, H, P])
        vnew = sb("v_new", [P, C])
        mask = sb("new_mask", [P, COLS])
        score = sb("scores", [P, 2, PAGES + 1, COLS])
        prob = sb("probs", [P, PAGES + 1, COLS])
        qcur = sb("q_current", [P, H, 2 * NEW])
        mpart, mall = sb("max_part", [P, COLS]), sb("max_all", [P, COLS])
        spart, sall = sb("sum_part", [P, 2, COLS]), sb("sum_all", [P, 2, COLS])
        srec = sb("sum_recip", [P, COLS])
        onorm = sb("o_normed", [P, COLS])
        oT = sb("o_turned", [P, H, NSEQ, NEW])
        orow = sb("o_rows", [TAIL, C])
        opad = sb("o_pad", [P - TAIL, C])
        tr = [ctx.enter_context(nc.psum_tensor(f"k_ps{n}", [P, 512], F32)) for n in range(4)]
        s_ps = [ctx.enter_context(nc.psum_tensor(f"s_ps{n}", [P, 512], F32)) for n in range(2)]
        new_ps = ctx.enter_context(nc.psum_tensor("new_ps", [P, 512], F32))
        o_ps = ctx.enter_context(nc.psum_tensor("od_ps", [P, 512], F32))
        k_in = sems(nc, ctx, *[f"k_page_in{x}" for x in range(4)])
        v_in = sems(nc, ctx, *[f"v_page_in{x}" for x in range(4)])
        (table_in, lane_ready, lane_step, row_ready, q_ready, zeroed, mask_zeroed, mask_ready, q_in, knew_in, vnew_in, k_turned, kt_dve, kt_act, scores_done, s_kept, new_ready,
         new_kept, max_part, max_ready, shifted, probs_ready, sum_part, sum_ready, pv_done, vnew_used, fin_step, o_kept,
         o_turned, o_row, o_stored) = sems(
            nc, ctx, "table_in", "lane_ready", "lane_step", "row_ready", "q_ready", "dec_zeroed", "mask_zeroed", "mask_ready", "q_in", "knew_in", "vnew_in", "k_turned", "kt_dve",
            "kt_act", "dec_scores", "s_kept", "new_ready", "new_kept", "max_part", "max_ready", "shifted", "probs_ready",
            "sum_part", "sum_ready", "dec_pv", "vnew_used", "fin_step", "dec_o_kept", "dec_o_turned", "dec_o_row",
            "dec_o_stored")
        PIECES = ROUNDS + 1
        TILES = PAGES + 1
        cache_k = g.cache_k[0].rearrange("n (l k) h d -> (n l) (k h d)", k=LOT)
        cache_v = g.cache_v[0].rearrange("n (l k) h d -> (n l) (k h d)", k=LOT)
        block = ctx.enter_context(nc.Block())

        def steps(eng, body):
            body(0, True, False, False)
            body(1, True, True, False)
            with eng.Fori(2, NSEQ) as b:
                body(b, True, True, True)
            body(NSEQ, False, True, True)
            body(NSEQ + 1, False, False, True)

        @block.sync
        def _(sp):
            sp.dma_start(table[:], g.page_table.rearrange("b n -> (b n)").partition_broadcast(P)).then_inc(table_in, 16)
            sp.wait_ge(zeroed, 4)
            for h in range(H):
                for m in range(2):
                    sp.dma_start(qz[m * HD:(m + 1) * HD, :, h, m * NEW:(m + 1) * NEW],
                                 g.qT[h, m * HD:(m + 1) * HD, SEQ:TOK].rearrange("p (b q) -> p b q", q=NEW)
                                 ).then_inc(q_in, 16)
            def body(b, scores, products, tail):
                if scores:
                    wait(sp, new_ready, b)
                    sp.dma_start(knew[:, :, 0:NEW], g.kT.rearrange("h p t -> p h t")[:, :, ds(b * NEW + SEQ, NEW)]
                                 ).then_inc(knew_in, 16)
                if products:
                    wait(sp, vnew_used, b - 1)
                    sp.dma_start(vnew[0:NEW, :], g.v_sample[ds((b - 1) * NEW, NEW), :]).then_inc(vnew_in, 16)

            steps(sp, body)
            sp.wait_ge(o_row, 1)
            sp.dma_start(g.attn[SEQ:TOK, :], orow[:]).then_inc(o_stored, 16)
            sp.dma_start(g.attn[TOK:TP, :], opad[:]).then_inc(o_stored, 16)
            sp.wait_ge(o_stored, 32)

        @block.tensor
        def _(pe):
            pe.wait_ge(zeroed, 4)

            def body(b, scores, products, tail):
                if scores:
                    pe.wait_ge(knew_in, 16 * b + 16)
                    pe.wait_ge(q_ready, b + 1)
                    for h in range(H):
                        mm = nc.tensor.matmul(new_ps[:, h * 2 * NEW:(h + 1) * 2 * NEW], knew[:, h, :],
                                              qcur[:, h, :], start=True, stop=True)
                    mm.then_inc(new_ready, 1)

                def turn(r, p):
                    if p % 4 == 0:
                        pe.wait_ge(k_in[p // LOT], (b * ROUNDS + r) * 16 + 16)
                    wait(pe, (kt_dve, kt_act)[p % 2], b * (PAGES // 2) + r * (ROUND // 2) + (p // 2 - 1))
                    for h in range(H):
                        mm = nc.tensor.transpose(tr[p % 4][:, h * P:(h + 1) * P], kpage[p][:, h * P:(h + 1) * P],
                                                 g.ident[:])
                    mm.then_inc(k_turned, 1)

                def score_page(r, p):
                    pe.wait_ge((kt_dve, kt_act)[p % 2], b * (PAGES // 2) + r * (ROUND // 2) + (p // 2 + 1))
                    if p % 8 == 0:
                        wait(pe, s_kept, b * 8 + r * 2 + (p // 8 - 1))
                    for h in range(H):
                        at = (p % 8) * COLS + h * 2 * NEW
                        mm = nc.tensor.matmul(s_ps[p // 8][:, at:at + 2 * NEW], kt[p % 4][:, h * P:(h + 1) * P],
                                              qcur[:, h, :], start=True, stop=True)
                    mm.then_inc(scores_done, 1)

                def product(c, r, p):
                    if p == 0:
                        pe.wait_ge(probs_ready, c * PIECES + (r + 2))
                    if r == 0 and p == 0:
                        pe.wait_ge(vnew_in, c * 16 + 16)
                        wait(pe, o_kept, c)
                        for h in range(H):
                            mm = nc.tensor.matmul(o_ps[:, h * 2 * NEW:(h + 1) * 2 * NEW], vnew[:, h * P:(h + 1) * P],
                                                  prob[:, PAGES, h * 2 * NEW:(h + 1) * 2 * NEW],
                                                  start=(h == 0), stop=False, skip_group_check=True)
                        mm.then_inc(vnew_used, 1)
                    if p % 4 == 0:
                        pe.wait_ge(v_in[p // LOT], (c * ROUNDS + r) * 16 + 16)
                    for h in range(H):
                        mm = nc.tensor.matmul(o_ps[:, h * 2 * NEW:(h + 1) * 2 * NEW], vpage[p][:, h * P:(h + 1) * P],
                                              prob[:, r * ROUND + p, h * 2 * NEW:(h + 1) * 2 * NEW],
                                              start=False, stop=False, skip_group_check=True)
                    mm.then_inc(pv_done, 1)

                for r in range(ROUNDS):
                    for p in range(ROUND + 2):
                        if scores and p < ROUND:
                            turn(r, p)
                        if scores and p >= 2:
                            score_page(r, p - 2)
                        if p >= 2 and r == 0 and tail:
                            product(b - 2, ROUNDS - 1, p - 2)
                        if p >= 2 and r and products:
                            product(b - 1, r - 1, p - 2)
            steps(pe, body)
            pe.wait_ge(o_kept, NSEQ)
            for h in range(H):
                mm = nc.tensor.transpose(new_ps[0:TAIL, h * P:(h + 1) * P], oT[:, h, :, :].rearrange("p b q -> p (b q)"),
                                         g.ident[:])
            mm.then_inc(o_turned, 1)

        @block.vector
        def _(dve):
            def body(b, scores, products, tail):
                if scores:
                    wait(dve, scores_done, b * PAGES)
                    nc.vector.tensor_copy(qcur[:], qz[:, ds(b, 1), :, :].rearrange("p a h q -> p (a h) q")
                                          ).then_inc(q_ready, 1)
                    dve.wait_ge(new_ready, b + 1)
                    if isinstance(b, int) and b == 0:
                        dve.wait_ge(mask_ready, 1)
                    wait(dve, probs_ready, (b - 1) * PIECES)
                    nc.vector.tensor_tensor(score[:, ds(b % 2, 1), PAGES, :].rearrange("p a c -> p (a c)"),
                                            new_ps[:, 0:COLS], mask[:], ALU.add).then_inc(new_kept, 1)

                def copy_page(r, p):
                    dve.wait_ge(k_turned, b * PAGES + r * ROUND + (p + 1))
                    wait(dve, scores_done, b * PAGES + r * ROUND + (p - 3))
                    nc.vector.tensor_copy(kt[p % 4][:], tr[p % 4][:]).then_inc(kt_dve, 1)

                def keep_scores(r, half):
                    dve.wait_ge(scores_done, b * PAGES + r * ROUND + 8 * (half + 1))
                    nc.vector.tensor_copy(
                        score[:, ds(b % 2, 1), ds(r * ROUND + 8 * half, 8), :].rearrange("p a t c -> p (a t c)"),
                        s_ps[half][:]).then_inc(s_kept, 1)

                def maxima():
                    dve.wait_ge(s_kept, 8 * b)
                    dve.wait_ge(new_kept, b)
                    nc.vector.tensor_reduce(
                        mpart[:], score[:, ds((b - 1) % 2, 1), :, :].rearrange("p a t c -> p c (a t)"), AX.X, ALU.max).then_inc(max_part, 1)

                def shift():
                    dve.wait_ge(max_ready, b)
                    s = score[:, ds((b - 1) % 2, 1), :, :].rearrange("p a t c -> p (a t) c")
                    nc.vector.tensor_tensor(s, s, mall[:].unsqueeze(1).to_broadcast([P, TILES, COLS]), ALU.subtract
                                            ).then_inc(shifted, 1)

                def sums():
                    dve.wait_ge(probs_ready, b * PIECES)
                    nc.vector.tensor_reduce(spart[:, ds((b - 1) % 2, 1), :].rearrange("p a c -> p (a c)"),
                                            prob[:].rearrange("p t c -> p c t"), AX.X, ALU.add
                                            ).then_inc(sum_part, 1)

                def finish():
                    dve.wait_ge(sum_ready, b - 1)
                    nc.vector.reciprocal(srec[:], sall[:, ds(b % 2, 1), :].rearrange("p a c -> p (a c)")
                                         ).then_inc(fin_step, 1)
                    dve.wait_ge(pv_done, (b - 1) * PAGES)
                    dve.wait_ge(fin_step, 2 * (b - 2) + 1)
                    nc.vector.tensor_tensor(onorm[:], o_ps[:, 0:COLS], srec[:], ALU.mult).then_inc(fin_step, 1)
                    dve.wait_ge(fin_step, 2 * (b - 2) + 2)
                    o = onorm[:].rearrange("p (h m q) -> p h m q", m=2, q=NEW)
                    nc.vector.scalar_tensor_tensor(out=oT[:, :, ds(b - 2, 1), :].rearrange("p h b q -> p h (b q)"),
                                                   in0=o[:, :, 1, :], scalar=g.neg_lam[:], in1=o[:, :, 0, :],
                                                   op0=ALU.mult, op1=ALU.add).then_inc(o_kept, 1)

                for r in range(ROUNDS):
                    if r == 0 and products:
                        maxima()
                        if not scores:
                            shift()
                    if scores:
                        for p in range(0, ROUND, 2):
                            copy_page(r, p)
                            if r == 0 and products and p == 6:
                                shift()
                            if p == 10:
                                keep_scores(r, 0)
                        keep_scores(r, 1)
                    if r == 0 and tail:
                        finish()
                    if r == 1 and products:
                        sums()
            dve.wait_ge(table_in, 16)
            dve.wait_ge(lane_ready, 1)
            for a in range(1, LOT):
                ins = nc.vector.tensor_scalar(lane[a * LANES:(a + 1) * LANES, :], lane[a * LANES:(a + 1) * LANES, :],
                                              -float(a * LANES), None, ALU.add).then_inc(lane_step, 1)
            dve.wait_ge(lane_step, LOT - 1)
            for a in range(LOT):
                at = slice(a * LANES, (a + 1) * LANES)
                nc.vector.tensor_scalar(row[at, :], table[at, :].rearrange("p (n a) -> p n a", a=LOT)[:, :, a],
                                        float(LANES), lane[at, :], ALU.mult, ALU.add).then_inc(row_ready, 1)
            dve.wait_ge(zeroed, 4)
            dve.wait_ge(q_in, 16 * 2 * H)
            steps(dve, body)
            dve.wait_ge(o_turned, 1)
            nc.vector.tensor_copy(orow[:], new_ps[0:TAIL, :]).then_inc(o_row, 1)

        @block.scalar
        def _(act):
            def body(b, scores, products, tail):
                def copy_page(r, p):
                    act.wait_ge(k_turned, b * PAGES + r * ROUND + (p + 1))
                    wait(act, scores_done, b * PAGES + r * ROUND + (p - 3))
                    nc.scalar.copy(kt[p % 4][:], tr[p % 4][:]).then_inc(kt_act, 1)

                def exponentials(n):
                    if n == 0:
                        act.wait_ge(shifted, b)
                        wait(act, sum_part, b - 1)
                        wait(act, vnew_used, b - 1)
                        tiles = slice(PAGES, PAGES + 1)
                    else:
                        wait(act, pv_done, (b - 2) * PAGES + n * ROUND if not isinstance(b, int) or b >= 2 else 0)
                        tiles = slice((n - 1) * ROUND, n * ROUND)
                    nc.scalar.activation(prob[:, tiles, :],
                                         score[:, ds((b - 1) % 2, 1), tiles, :].rearrange("p a t c -> p (a t) c"),
                                         ACT.Exp, scale=SCALE).then_inc(probs_ready, 1)

                for r in range(ROUNDS):
                    for p in range(1, ROUND, 2):
                        if scores:
                            copy_page(r, p)
                        if products:
                            for n in {(0, 7): (0, 1), (0, 11): (2,), (0, 15): (3,), (1, 5): (4,)}.get((r, p), ()):
                                exponentials(n)
            steps(act, body)

        @block.gpsimd
        def _(pool):
            for t in (qz, knew, vnew, opad):
                nc.gpsimd.memset(t[:], 0.0).then_inc(zeroed, 1)
            nc.gpsimd.memset(mask[:], 0.0).then_inc(mask_zeroed, 1)
            pool.wait_ge(mask_zeroed, 1)
            nc.gpsimd.affine_select(out=mask[:].rearrange("p (c q) -> p c q", q=NEW),
                                    in_=mask[:].rearrange("p (c q) -> p c q", q=NEW), compare_op=ALU.is_ge, fill=NEG,
                                    base=0, pattern=[[0, 2 * H], [1, NEW]], channel_multiplier=-1
                                    ).then_inc(mask_ready, 1)
            nc.gpsimd.iota(lane[:], pattern=[[0, 1]], base=0, channel_multiplier=1,
                           allow_small_or_imprecise_dtypes=True).then_inc(lane_ready, 1)

            def gather(x, to, arrived, cache, c, r, freed):
                wait(pool, freed, c * PAGES + r * ROUND + (LOT * x + LOT - ROUND))
                n = (c * ROUNDS + r) * LOTS + x
                pool.indirect_dma_start(
                    out=to[x][:].rearrange("p k c -> p (k c)"), out_offset=None, in_=cache,
                    in_offset=bass.IndirectOffsetOnAxis(ap=row[:, n:n + 1], axis=0)).then_inc(arrived[x], 16)

            pool.wait_ge(row_ready, LOT)
            for b in range(NSEQ + 2):
                for r in range(ROUNDS):
                    for x in range(LOTS):
                        if b < NSEQ:
                            gather(x, klot, k_in, cache_k, b, r, k_turned)
                        if r == 0 and b >= 2:
                            gather(x, vlot, v_in, cache_v, b - 2, ROUNDS - 1, pv_done)
                        if r and 1 <= b <= NSEQ:
                            gather(x, vlot, v_in, cache_v, b - 1, r - 1, pv_done)
                    if r == 0 and 1 <= b <= NSEQ:
                        pool.wait_ge(max_part, b)
                        nc.gpsimd.partition_all_reduce(mall[:], mpart[:], P, bass.bass_isa.ReduceOp.max
                                                       ).then_inc(max_ready, 1)
                    if r == 2 and 1 <= b <= NSEQ:
                        pool.wait_ge(sum_part, b)
                        nc.gpsimd.partition_all_reduce(sall[:, (b - 1) % 2, :], spart[:, (b - 1) % 2, :], P,
                                                       bass.bass_isa.ReduceOp.add).then_inc(sum_ready, 1)


ALPHA = 2.0 ** 0.25
E = 64
EG = 8
TOPG = 4
TOPK = 8
ROUTED_SCALE = 2.5


def tile_pipeline(eng, body):
    body(-1, True, False, False)
    body(0, True, True, False)
    with eng.Fori(1, TT - 1) as t:
        body(t, True, True, True)
    body(TT - 1, False, True, True)
    body(TT, False, False, True)


def mix_and_route(nc, g):
    with ExitStack() as ctx:
        sb = lambda n, s, dt=F32: ctx.enter_context(nc.sbuf_tensor(n, s, dt))
        wo = sb("w_o", [P, KT, D])
        wr = sb("w_router", [P, KT, E])
        ln_g, ln_b = sb("ln1_g", [P, D]), sb("ln1_b", [P, D])
        cg, cb = sb("conv_g", [P, C]), sb("conv_b", [P, C])
        sub = sb("subln", [P, P])
        br = sb("b_router", [P, E])
        o_in, c_in, x_in = sb("o_in", [P, C]), sb("c_in", [P, H, P]), sb("x_res", [P, D])
        mix, mT = sb("mix", [P, D]), sb("mixT", [P, KT, P])
        res, x1, x1T = sb("residual", [P, D]), sb("x1", [P, D]), sb("x1T", [P, KT, P])
        square = sb("square", [P, C])
        rms, rstd = sb("rms", [P, H]), sb("rms_rstd", [P, H])
        cst, cmv, crs, cn = sb("c_stats", [P, 6]), sb("c_meanvar", [P, 2]), sb("c_rstd", [P, 2]), sb("c_norm", [P, C])
        lst, lmv, lrs = sb("l_stats", [P, 2, 6]), sb("l_meanvar", [P, 2]), sb("l_rstd", [P, 2])
        sig, sel, srt = sb("sigmoids", [P, E]), sb("selection", [P, E]), sb("group_sorted", [P, EG, 8])
        gs, g8, gi, gf = (sb("group_score", [P, EG]), sb("group_top", [P, 8]), sb("group_index", [P, 8], U32),
                          sb("group_index_f", [P, 8]))
        eq, gm, pen = sb("group_hits", [P, EG, TOPG]), sb("group_mask", [P, EG]), sb("group_penalty", [P, EG])
        v8, picked, hit = sb("top_values", [P, 8]), sb("picked", [P, E]), sb("hits", [P, E])
        w, ws, wrec = sb("raw_weights", [P, E]), sb("weight_sum", [P, 1]), sb("weight_recip", [P, 1])
        eps = sb("eps", [P, 1])
        bank = lambda n: ctx.enter_context(nc.psum_tensor(n, [P, 512], F32))
        c_ps, r_ps = bank("c_ps"), bank("router_ps")
        m_ps, p_ps, x_ps = ([bank(f"{n}{i}") for i in range(2)] for n in ("mix_ps", "proj_ps", "x1_ps"))
        (w_in, eps_ready, o_arr, c_arr, x_arr, c_turned, m_turned, m_copied, projected, x_turned, x_copied, routed,
         n_step, a_step, l_step, l_root, r_sig, r_step, x1_out) = sems(
            nc, ctx, "p4_w_in", "eps_ready", "o_arrived", "c_arrived", "x_arrived", "c_turned", "m_turned", "m_copied",
            "projected", "x1_turned", "x1_copied", "routed", "norm_step", "norm_act", "ln_step", "ln_root",
            "sig_ready", "route_step", "x1_out")
        block = ctx.enter_context(nc.Block())
        NS, AS, LS, RS = 10, 5, 8, 25

        @block.sync
        def _(sp):
            for dst, src in ((wo[:], g.w_o[0].rearrange("(k p) n -> p k n", p=P)),
                             (wr[:], g.w_router[0].rearrange("(k p) n -> p k n", p=P)),
                             (ln_g[:], g.ln1_g[0].partition_broadcast(P)), (ln_b[:], g.ln1_b[0].partition_broadcast(P)),
                             (cg[:], g.conv_ln_g[0].partition_broadcast(P)),
                             (cb[:], g.conv_ln_b[0].partition_broadcast(P)),
                             (sub[:], g.subln_g[0].partition_broadcast(P)),
                             (br[:], g.b_router[0].partition_broadcast(P))):
                sp.dma_start(dst, src).then_inc(w_in, 16)

            def body(t, mixes, projects, routes):
                if mixes:
                    held(sp, n_step, (t + 1) * NS, g.passed)
                    held(sp, a_step, (t + 1) * AS, g.passed)
                    sp.dma_start(o_in[:], g.attn[ds((t + 1) * P, P), :]).then_inc(o_arr, 16)
                    held(sp, c_turned, t + 1, g.passed)
                    sp.dma_start(c_in[:], g.convT.rearrange("i p t -> p i t")[:, :, ds((t + 1) * P, P)]
                                 ).then_inc(c_arr, 16)
                if projects:
                    wait(sp, l_step, (t - 1) * LS + 2)
                    if isinstance(t, int) and t == TT - 1:
                        sp.dma_start(x_in[:], g.x_tail).then_inc(x_arr, 16)
                    else:
                        sp.dma_start(x_in[:], g.x_prompt[ds(t * P, P), :]).then_inc(x_arr, 16)
                    sp.wait_ge(l_step, (t + 1) * LS)
                    sp.dma_start(g.x1[ds(t * P, P), :], x1[:]).then_inc(x1_out, 16)
            tile_pipeline(sp, body)
            sp.wait_ge(x1_out, 16 * TT)

        @block.tensor
        def _(pe):
            pe.wait_ge(w_in, 16 * 8)

            def body(t, mixes, projects, routes):
                if mixes:
                    pe.wait_ge(c_arr, (t + 1) * 16 + 16)
                    wait(pe, n_step, (t + 1) * NS)
                    for i in range(H):
                        mm = nc.tensor.transpose(c_ps[:, i * P:(i + 1) * P], c_in[:, i, :], g.ident[:])
                    mm.then_inc(c_turned, 1)
                if projects:
                    pe.wait_ge(n_step, (t + 1) * NS)
                    pe.wait_ge(a_step, (t + 1) * AS)
                    for half in range(2):
                        for k in range(4):
                            kk = 4 * half + k
                            mm = nc.tensor.transpose(m_ps[half][:, k * P:(k + 1) * P], mix[:, kk * P:(kk + 1) * P],
                                                     g.ident[:])
                        mm.then_inc(m_turned, 1)
                    pe.wait_ge(m_copied, t * 2 + 2)
                    wait(pe, l_step, (t - 1) * LS + 2)
                    for half in range(2):
                        for k in range(KT):
                            mm = nc.tensor.matmul(p_ps[half][:], mT[:, k, :], wo[:, k, half * 512:(half + 1) * 512],
                                                  start=(k == 0), stop=(k == KT - 1))
                        mm.then_inc(projected, 1)
                if routes:
                    pe.wait_ge(l_step, t * LS)
                    wait(pe, x_copied, (t - 1) * 2)
                    for half in range(2):
                        for k in range(4):
                            kk = 4 * half + k
                            mm = nc.tensor.transpose(x_ps[half][:, k * P:(k + 1) * P], x1[:, kk * P:(kk + 1) * P],
                                                     g.ident[:])
                        mm.then_inc(x_turned, 1)
                    pe.wait_ge(x_copied, t * 2)
                    wait(pe, r_sig, t - 1)
                    for k in range(KT):
                        mm = nc.tensor.matmul(r_ps[:, 0:E], x1T[:, k, :], wr[:, k, :], start=(k == 0),
                                              stop=(k == KT - 1))
                    mm.then_inc(routed, 1)
            tile_pipeline(pe, body)

        @block.scalar
        def _(act):
            act.wait_ge(eps_ready, 1)

            def body(t, mixes, projects, routes):
                if projects:
                    for half in range(2):
                        act.wait_ge(m_turned, t * 2 + (half + 1))
                        nc.scalar.copy(mT[:, 4 * half:4 * half + 4, :],
                                       m_ps[half][:].rearrange("p (k t) -> p k t", k=4)).then_inc(m_copied, 1)
                if mixes:
                    act.wait_ge(o_arr, (t + 1) * 16 + 16)
                    wait(act, n_step, (t + 1) * NS)
                    for h in range(H):
                        ins = nc.scalar.activation(square[:, h * P:(h + 1) * P], o_in[:, h * P:(h + 1) * P], ACT.Square,
                                                   accum_out=rms[:, h:h + 1])
                        if h == H - 1:
                            ins.then_inc(a_step, 1)
                    act.wait_ge(a_step, (t + 1) * AS + 1)
                    nc.scalar.activation(rms[:], rms[:], ACT.Sqrt, bias=eps[:], scale=1.0 / P).then_inc(a_step, 1)
                    act.wait_ge(n_step, (t + 1) * NS + 2)
                    nc.scalar.activation(crs[:, 0:1], cmv[:, 1:2], ACT.Sqrt, bias=eps[:]).then_inc(a_step, 1)
                    act.wait_ge(n_step, (t + 1) * NS + 6)
                    wait(act, m_turned, (t + 1) * 2)
                    nc.scalar.activation(mix[:, C:D], cn[:], ACT.Silu).then_inc(a_step, 2)
                if routes:
                    for half in range(2):
                        act.wait_ge(x_turned, (t - 1) * 2 + (half + 1))
                        wait(act, routed, t - 1)
                        nc.scalar.copy(x1T[:, 4 * half:4 * half + 4, :],
                                       x_ps[half][:].rearrange("p (k t) -> p k t", k=4)).then_inc(x_copied, 1)
                if projects:
                    act.wait_ge(l_step, t * LS + 4)
                    nc.scalar.activation(lrs[:, 0:1], lmv[:, 1:2], ACT.Sqrt, bias=eps[:]).then_inc(l_root, 1)
                if routes:
                    act.wait_ge(routed, t)
                    wait(act, r_step, (t - 1) * RS)
                    nc.scalar.activation(sig[:], r_ps[:, 0:E], ACT.Sigmoid).then_inc(r_sig, 1)
            tile_pipeline(act, body)

        @block.vector
        def _(dve):
            nc.vector.memset(eps[:], EPS).then_inc(eps_ready, 1)
            dve.wait_ge(w_in, 16 * 8)
            nc.vector.tensor_scalar(sub[:], sub[:], 1.0 - LAMBDA_INIT, None, ALU.mult).then_inc(eps_ready, 1)
            dve.wait_ge(eps_ready, 2)

            def norms(t):
                b = t * NS
                dve.wait_ge(c_turned, t + 1)
                nc.vector.bn_stats(cst[:], c_ps[:]).then_inc(n_step, 1)
                held(dve, n_step, b + 1, g.passed)
                nc.vector.bn_aggr(cmv[:], cst[:]).then_inc(n_step, 1)
                dve.wait_ge(a_step, t * AS + 3)
                nc.vector.reciprocal(crs[:, 1:2], crs[:, 0:1]).then_inc(n_step, 1)
                dve.wait_ge(n_step, b + 3)
                nc.vector.tensor_scalar(cn[:], c_ps[:], cmv[:, 0:1], crs[:, 1:2], ALU.subtract, ALU.mult
                                        ).then_inc(n_step, 1)
                dve.wait_ge(n_step, b + 4)
                nc.vector.tensor_tensor(cn[:], cn[:], cg[:], ALU.mult).then_inc(n_step, 1)
                dve.wait_ge(n_step, b + 5)
                nc.vector.tensor_tensor(cn[:], cn[:], cb[:], ALU.add).then_inc(n_step, 1)
                nc.vector.reciprocal(rstd[:], rms[:]).then_inc(n_step, 1)
                dve.wait_ge(n_step, b + 7)
                wait(dve, m_turned, t * 2)
                for h in range(H):
                    ins = nc.vector.scalar_tensor_tensor(out=mix[:, h * P:(h + 1) * P], in0=o_in[:, h * P:(h + 1) * P],
                                                         scalar=rstd[:, h:h + 1], in1=sub[:], op0=ALU.mult,
                                                         op1=ALU.mult)
                ins.then_inc(n_step, 3)

            def layer_norm(t):
                b = t * LS
                dve.wait_ge(x_arr, t * 16 + 16)
                for half in range(2):
                    dve.wait_ge(projected, t * 2 + (half + 1))
                    at = slice(half * 512, (half + 1) * 512)
                    nc.vector.scalar_tensor_tensor(out=res[:, at], in0=x_in[:, at], scalar=ALPHA, in1=p_ps[half][:],
                                                   op0=ALU.mult, op1=ALU.add).then_inc(l_step, 1)
                for half in range(2):
                    dve.wait_ge(l_step, b + (half + 1))
                    ins = nc.vector.bn_stats(lst[:, half, :], res[:, half * 512:(half + 1) * 512])
                ins.then_inc(l_step, 1)
                held(dve, l_step, b + 3, g.passed)
                nc.vector.bn_aggr(lmv[:], lst[:].rearrange("p a b -> p (a b)")).then_inc(l_step, 1)
                dve.wait_ge(l_root, t + 1)
                nc.vector.reciprocal(lrs[:, 1:2], lrs[:, 0:1]).then_inc(l_step, 1)
                dve.wait_ge(l_step, b + 5)
                nc.vector.tensor_scalar(res[:], res[:], lmv[:, 0:1], lrs[:, 1:2], ALU.subtract, ALU.mult
                                        ).then_inc(l_step, 1)
                dve.wait_ge(l_step, b + 6)
                nc.vector.tensor_tensor(res[:], res[:], ln_g[:], ALU.mult).then_inc(l_step, 1)
                dve.wait_ge(l_step, b + 7)
                wait(dve, x_turned, t * 2)
                wait(dve, x1_out, t * 16)
                nc.vector.tensor_tensor(x1[:], res[:], ln_b[:], ALU.add).then_inc(l_step, 1)

            def route(t):
                n = [0]

                def step(ins):
                    ins.then_inc(r_step, 1)
                    n[0] += 1

                def settled():
                    held(dve, r_step, t * RS + n[0], g.passed)
                dve.wait_ge(r_sig, t + 1)
                step(nc.vector.tensor_tensor(sel[:], sig[:], br[:], ALU.add))
                settled()
                for k in range(EG):
                    step(nc.vector.max(out=srt[:, k, :], in_=sel[:, k * EG:(k + 1) * EG]))
                settled()
                step(nc.vector.tensor_tensor(gs[:], srt[:, :, 0], srt[:, :, 1], ALU.add))
                settled()
                step(nc.vector.max(out=g8[:], in_=gs[:]))
                settled()
                step(nc.vector.max_index(out=gi[:], in_max=g8[:], in_values=gs[:]))
                settled()
                step(nc.vector.tensor_copy(gf[:], gi[:]))
                settled()
                step(nc.vector.tensor_tensor(eq[:], g.iota_e[:, 0:EG].unsqueeze(2).to_broadcast([P, EG, TOPG]),
                                             gf[:, 0:TOPG].unsqueeze(1).to_broadcast([P, EG, TOPG]), ALU.is_equal))
                settled()
                step(nc.vector.tensor_reduce(gm[:], eq[:], AX.X, ALU.add))
                settled()
                step(nc.vector.tensor_scalar(pen[:], gm[:], -1.0, -NEG, ALU.add, ALU.mult))
                step(nc.vector.tensor_tensor(sel[:].rearrange("p (g e) -> p g e", g=EG),
                                             sel[:].rearrange("p (g e) -> p g e", g=EG),
                                             gm[:].unsqueeze(2).to_broadcast([P, EG, E // EG]), ALU.mult))
                settled()
                step(nc.vector.tensor_tensor(sel[:].rearrange("p (g e) -> p g e", g=EG),
                                             sel[:].rearrange("p (g e) -> p g e", g=EG),
                                             pen[:].unsqueeze(2).to_broadcast([P, EG, E // EG]), ALU.add))
                settled()
                step(nc.vector.max(out=v8[:], in_=sel[:]))
                settled()
                step(nc.vector.match_replace(out=picked[:], in_to_replace=v8[:], in_values=sel[:], imm_value=-NEG))
                settled()
                step(nc.vector.tensor_scalar(hit[:], picked[:], -NEG, None, ALU.is_equal))
                settled()
                step(nc.vector.scalar_tensor_tensor(out=w[:], in0=sig[:], scalar=1.0, in1=hit[:], op0=ALU.mult,
                                                    op1=ALU.mult, accum_out=ws[:]))
                step(nc.vector.tensor_scalar(g.chosen[:, ds(t, 1), :].rearrange("p a e -> p (a e)"), hit[:],
                                             g.valid[:, ds(t, 1)], None, ALU.mult))
                settled()
                step(nc.vector.reciprocal(wrec[:], ws[:]))
                settled()
                step(nc.vector.tensor_scalar(g.weight[:, ds(t, 1), :].rearrange("p a e -> p (a e)"), w[:], wrec[:],
                                             ROUTED_SCALE, ALU.mult, ALU.mult))
                assert n[0] == RS, n[0]

            def body(t, mixes, projects, routes):
                if mixes:
                    norms(t + 1)
                if projects:
                    layer_norm(t)
                if routes:
                    route(t - 1)
            tile_pipeline(dve, body)


SH = TT
SLOTS = TOK * TOPK
NBLK = SH + (SLOTS + E * P) // P + 1


def plan_dispatch(nc, g):
    with ExitStack() as ctx:
        sb = lambda n, s, dt=F32: ctx.enter_context(nc.sbuf_tensor(n, s, dt))
        bf = sb("chosen_bf", [P, TT, E], BF16)
        tri, ones = sb("earlier", [P, P], BF16), sb("ones_bf", [P, P], BF16)
        before = sb("before_tile", [P, TT + 1, E])
        count_i, blocks, one = sb("count_int", [P, E], I32), sb("blocks", [P, E]), sb("ones_row", [P, E])
        upto, base = sb("blocks_upto", [P, E]), sb("base_row", [P, E])
        rowno = sb("row_plus1", [P, TT, E])
        d8 = sb("row8_f", [P, TT, TOPK])
        match = sb("match", [P, TT, TOPK, E])
        lo, hi = sb("row_low", [P, TT * TOPK], I32), sb("row_high", [P, TT * TOPK], I32)
        zero_table = sb("zero_table", [P, NBLK], U32)
        chunks = [(0, 8), (8, 8), (16, 1)]
        r_ps = [ctx.enter_context(nc.psum_tensor(f"rank_ps{c}", [P, 512], F32)) for c in range(3)]
        c_ps = [ctx.enter_context(nc.psum_tensor(f"count_ps{c}", [P, 512], F32)) for c in range(3)]
        const_ready, bf_ready, ranked, step, table_out = sems(nc, ctx, "pd_const", "pd_bf", "pd_ranked", "pd_step",
                                                             "table_out")
        block = ctx.enter_context(nc.Block())

        @block.gpsimd
        def _(pool):
            nc.gpsimd.memset(zero_table[:], 0).then_inc(const_ready, 1)
            nc.gpsimd.memset(ones[:], 1.0).then_inc(const_ready, 1)
            nc.gpsimd.memset(tri[:], 1.0).then_inc(const_ready, 1)
            pool.wait_ge(const_ready, 3)
            nc.gpsimd.affine_select(out=tri[:], in_=tri[:], compare_op=ALU.is_gt, fill=0.0, base=0,
                                    pattern=[[1, P]], channel_multiplier=-1).then_inc(const_ready, 1)
            pool.dma_start(g.slot_token.rearrange("(p b) -> p b", p=P), zero_table[:]).then_inc(table_out, 16)
            pool.wait_ge(table_out, 16)

        @block.tensor
        def _(pe):
            pe.wait_ge(const_ready, 4)
            pe.wait_ge(bf_ready, 1)
            for ps, lhs in ((c_ps, ones), (r_ps, tri)):
                for c, (t, n) in enumerate(chunks):
                    nc.tensor.matmul(ps[c][:, 0:n * E], lhs[:], bf[:, t:t + n, :].rearrange("p t e -> p (t e)"),
                                     start=True, stop=True).then_inc(ranked, 1)

        @block.vector
        def _(dve):
            n = [0]

            def then(ins):
                ins.then_inc(step, 1)
                n[0] += 1
                dve.wait_ge(step, n[0])
            nc.vector.tensor_copy(bf[:], g.chosen[:]).then_inc(bf_ready, 1)
            then(nc.vector.memset(one[:], 1.0))
            then(nc.vector.memset(before[:, 0, :], 0.0))
            dve.wait_ge(ranked, 3)
            for t in range(TT):
                then(nc.vector.tensor_tensor(before[:, t + 1, :], before[:, t, :],
                                             c_ps[t // 8][:, (t % 8) * E:(t % 8 + 1) * E], ALU.add))
            then(nc.vector.tensor_scalar(count_i[:], before[:, TT, :], float(P - 1), None, ALU.add))
            then(nc.vector.tensor_scalar(count_i[:], count_i[:], 7, None, ALU.logical_shift_right))
            then(nc.vector.tensor_scalar(blocks[:], count_i[:], 1.0, None, ALU.max))
            then(nc.vector.tensor_tensor_scan(upto[:], one[:], blocks[:], float(SH), ALU.mult, ALU.add))
            then(nc.vector.memset(g.bounds[:, 0:1], SH))
            then(nc.vector.tensor_copy(g.bounds[:, 1:E + 1], upto[0:1, :]))
            then(nc.vector.tensor_scalar(g.bounds[:, E + 1:E + 2], upto[0:1, E - 1:E], -1.0, float(NBLK), ALU.mult,
                                         ALU.add))
            then(nc.vector.tensor_tensor(base[:], upto[:], blocks[:], ALU.subtract))
            then(nc.vector.tensor_scalar(base[:], base[:], float(P), 1.0, ALU.mult, ALU.add))
            dve.wait_ge(ranked, 6)
            for c, (t, m) in enumerate(chunks):
                then(nc.vector.tensor_tensor(rowno[:, t:t + m, :], before[:, t:t + m, :],
                                             r_ps[c][:, 0:m * E].rearrange("p (t e) -> p t e", e=E), ALU.add))
            then(nc.vector.tensor_tensor(rowno[:], rowno[:], base[:].unsqueeze(1).to_broadcast([P, TT, E]), ALU.add))
            then(nc.vector.tensor_tensor(rowno[:], rowno[:], g.chosen[:], ALU.mult))
            for t in range(TT):
                ins = nc.vector.max(out=d8[:, t, :], in_=rowno[:, t, :])
            then(ins)
            b4 = [P, TT, TOPK, E]
            then(nc.vector.tensor_tensor(match[:], rowno[:].unsqueeze(2).to_broadcast(b4),
                                         d8[:].unsqueeze(3).to_broadcast(b4), ALU.is_equal))
            then(nc.vector.tensor_tensor(match[:], match[:], g.weight[:].unsqueeze(2).to_broadcast(b4), ALU.mult))
            then(nc.vector.tensor_reduce(g.weight8[:], match[:], AX.X, ALU.add))
            then(nc.vector.tensor_scalar(g.row8[:], d8[:], -1.0, None, ALU.add))
            r = g.row8[:].rearrange("p t k -> p (t k)")
            then(nc.vector.tensor_scalar(lo[:], r, P - 1, None, ALU.bitwise_and))
            then(nc.vector.tensor_scalar(hi[:], r, 7, None, ALU.arith_shift_right))
            then(nc.vector.scalar_tensor_tensor(out=g.place8[:].rearrange("p t k -> p (t k)"), in0=lo[:],
                                                scalar=float(NBLK), in1=hi[:], op0=ALU.mult, op1=ALU.add))


F = 256


def experts(nc, g):
    with ExitStack() as ctx:
        sb = lambda n, s, dt=F32: ctx.enter_context(nc.sbuf_tensor(n, s, dt))
        token = sb("token_no", [P, TT], U32)
        index = sb("gather_index", [P, NBLK + 1], U32)
        now = sb("gather_now", [P, 1], U32)
        wgu = [sb(f"w_gate_up{u}", [P, 2, KT, F]) for u in range(2)]
        wd = [sb(f"w_down{u}", [P, F // P, D]) for u in range(2)]
        xg, xT = sb("x_rows", [P, D]), sb("x_rowsT", [P, KT, P])
        sg, hid, hT, y = sb("silu_gate", [P, F]), sb("hidden", [P, F]), sb("hiddenT", [P, F // P, P]), sb("y_rows", [P, D])
        zero = sb("zero_rows", [P, D])
        bank = lambda n: ctx.enter_context(nc.psum_tensor(n, [P, 512], F32))
        g_ps, u_ps, h_ps = bank("gate_ps"), bank("up_ps"), bank("hid_ps")
        x_ps, y_ps = [bank(f"xr_ps{i}") for i in range(2)], [bank(f"y_ps{i}") for i in range(2)]
        (token_ready, scattered, index_ready, now_ready, x_arr, x_turned, xt_act, xt_dve, w_arr0, w_arr1, picked_ready, gated, upped,
         silu_ready, h_ready, h_turned, h_copied, downed, y_act, y_dve, y_out, zero_ready, filled) = sems(
            nc, ctx, "token_ready", "scattered", "index_ready", "now_ready", "xr_arrived", "xr_turned", "xr_act", "xr_dve",
            "we_arrived0", "we_arrived1", "picked_ready", "gated", "upped", "silu_ready", "h_ready", "h_turned", "h_copied",
            "downed", "y_act", "y_dve", "y_out", "zero_ready", "filled")
        w_arr = (w_arr0, w_arr1)
        W_DMAS = 3 * 16

        def blocks(eng, block, begin=lambda i, u, lower: None):
            block(0, 0)
            with eng.Fori(1, SH - 2) as n:
                block(n, 0)
            block(SH - 2, 0)
            block(SH - 1, 0)

            def pair(i):
                for u in (1, 0):
                    _, (lower, upper) = nc.values_load_multi_w_load_instructions(
                        g.bounds[0:1, ds(i * 2 + (1 - u), 2)], (eng.engine,), min_val=SH, max_val=NBLK - 1)
                    begin(i, u, lower)
                    with eng.Fori(lower, upper) as n:
                        block(n, u)
            with eng.Fori(0, E // 2 - 1) as i:
                pair(i)
            pair(E // 2 - 1)

        block = ctx.enter_context(nc.Block())

        @block.sync
        def _(sp):
            def load(u, gate, up, down):
                sp.dma_start(wgu[u][:, 0, :, :], gate.rearrange("(k p) f -> p k f", p=P)).then_inc(w_arr[u], 16)
                sp.dma_start(wgu[u][:, 1, :, :], up.rearrange("(k p) f -> p k f", p=P)).then_inc(w_arr[u], 16)
                sp.dma_start(wd[u][:], down.rearrange("(k p) n -> p k n", p=P)).then_inc(w_arr[u], 16)

            load(0, g.w_sh_gate[0], g.w_sh_up[0], g.w_sh_down[0])
            load(1, g.w_gate[0, 0], g.w_up[0, 0], g.w_down[0, 0])
            _, (last,) = nc.values_load_multi_w_load_instructions(g.bounds[0:1, E:E + 1], (sp.engine,), min_val=SH,
                                                                  max_val=NBLK - 1)
            sp.wait_ge(zero_ready, 1)
            with sp.Fori(last, NBLK) as n:
                sp.dma_start(g.y[ds(n * P, P), :], zero[:]).then_inc(filled, 16)

            def begin(i, u, lower):
                if isinstance(i, int) and u == 0:
                    return
                held(sp, downed, lower * 2, g.passed)
                load(1 - u, *(t[0][ds(i * 2 + (2 - u), 1)].rearrange("a r c -> (a r) c")
                              for t in (g.w_gate, g.w_up, g.w_down)))

            def store(n, u):
                sp.wait_ge(y_act, n + 1)
                sp.wait_ge(y_dve, n + 1)
                sp.dma_start(g.y[ds(n * P, P), :], y[:]).then_inc(y_out, 16)
            blocks(sp, store, begin)
            held(sp, y_out, last * 16, g.passed)
            _, (unused,) = nc.values_load_multi_w_load_instructions(g.bounds[0:1, E + 1:E + 2], (sp.engine,),
                                                                    min_val=1, max_val=NBLK)
            held(sp, filled, unused * 16, g.passed)

        @block.gpsimd
        def _(pool):
            nc.gpsimd.iota(token[:], pattern=[[P, TT]], base=0, channel_multiplier=1).then_inc(token_ready, 1)
            nc.gpsimd.memset(index[:, NBLK:NBLK + 1], 0).then_inc(token_ready, 1)
            pool.wait_ge(token_ready, 2)

            def gather(n):
                held(pool, now_ready, n + 1, g.passed)
                pool.indirect_dma_start(out=xg[:], out_offset=None, in_=g.x1,
                                        in_offset=bass.IndirectOffsetOnAxis(ap=now[:], axis=0)).then_inc(x_arr, 16)

            for n in range(SH):
                gather(n)
                rows = P if n < QT else TAIL
                for k in range(TOPK):
                    pool.indirect_dma_start(
                        out=g.slot_token.rearrange("(s a) -> s a", a=1),
                        out_offset=bass.IndirectOffsetOnAxis(ap=g.place8[0:rows, n, k:k + 1], axis=0),
                        in_=token[0:rows, n:n + 1], in_offset=None).then_inc(scattered, 16)
            pool.wait_ge(scattered, 16 * SH * TOPK)
            pool.dma_start(index[:, SH:NBLK], g.slot_token.rearrange("(p b) -> p b", p=P)[:, SH:NBLK]
                           ).then_inc(index_ready, 16)
            _, (last,) = nc.values_load_multi_w_load_instructions(g.bounds[0:1, E:E + 1], (pool.engine,), min_val=SH,
                                                                  max_val=NBLK - 1)
            with pool.Fori(SH, last + 1) as n:
                gather(n)

        @block.tensor
        def _(pe):
            def turn(n):
                pe.wait_ge(x_arr, n * 16 + 16)
                for half in range(2):
                    for k in range(4):
                        kk = 4 * half + k
                        mm = nc.tensor.transpose(x_ps[half][:, k * P:(k + 1) * P], xg[:, kk * P:(kk + 1) * P],
                                                 g.ident[:])
                    mm.then_inc(x_turned, 1)
            turn(0)

            def products(n, u):
                pe.wait_ge(xt_act, n + 1)
                pe.wait_ge(xt_dve, n + 1)
                for ps, which, done in ((g_ps, 0, gated), (u_ps, 1, upped)):
                    for k in range(KT):
                        mm = nc.tensor.matmul(ps[:, 0:F], xT[:, k, :], wgu[u][:, which, k, :], start=(k == 0),
                                              stop=(k == KT - 1))
                    mm.then_inc(done, 1)
                turn(n + 1)
                pe.wait_ge(h_ready, n + 1)
                for k in range(F // P):
                    mm = nc.tensor.transpose(h_ps[:, k * P:(k + 1) * P], hid[:, k * P:(k + 1) * P], g.ident[:])
                mm.then_inc(h_turned, 1)
                pe.wait_ge(h_copied, n + 1)
                for half, kept in ((0, y_act), (1, y_dve)):
                    wait(pe, kept, n)
                    for k in range(F // P):
                        mm = nc.tensor.matmul(y_ps[half][:], hT[:, k, :], wd[u][:, k, half * 512:(half + 1) * 512],
                                              start=(k == 0), stop=(k == F // P - 1))
                    mm.then_inc(downed, 1)

            def begin(i, u, lower):
                held(pe, w_arr[u], i * W_DMAS + (W_DMAS if u else 2 * W_DMAS), g.passed)
            pe.wait_ge(w_arr[0], W_DMAS)
            blocks(pe, products, begin)

        @block.scalar
        def _(act):
            def turned(n):
                act.wait_ge(x_turned, n * 2 + 1)
                nc.scalar.copy(xT[:, 0:4, :], x_ps[0][:].rearrange("p (k t) -> p k t", k=4)).then_inc(xt_act, 1)
            turned(0)

            def body(n, u):
                act.wait_ge(gated, n + 1)
                wait(act, h_ready, n)
                nc.scalar.activation(sg[:], g_ps[:, 0:F], ACT.Silu).then_inc(silu_ready, 1)
                turned(n + 1)
                act.wait_ge(downed, n * 2 + 1)
                wait(act, y_out, n * 16)
                nc.scalar.copy(y[:, 0:512], y_ps[0][:]).then_inc(y_act, 1)
            blocks(act, body)

        @block.vector
        def _(dve):
            def pick(n):
                nc.vector.tensor_copy(now[:], index[:, ds(n, 1)]).then_inc(now_ready, 1)

            def turned(n):
                dve.wait_ge(x_turned, n * 2 + 2)
                nc.vector.tensor_copy(xT[:, 4:8, :], x_ps[1][:].rearrange("p (k t) -> p k t", k=4)).then_inc(xt_dve, 1)
            dve.wait_ge(token_ready, 2)
            nc.vector.memset(zero[:], 0.0).then_inc(zero_ready, 1)
            nc.vector.tensor_copy(index[:, 0:SH], token[:]).then_inc(picked_ready, 1)
            dve.wait_ge(picked_ready, 1)
            pick(0)
            turned(0)
            pick(1)

            def body(n, u):
                dve.wait_ge(silu_ready, n + 1)
                dve.wait_ge(upped, n + 1)
                nc.vector.tensor_tensor(hid[:], sg[:], u_ps[:, 0:F], ALU.mult).then_inc(h_ready, 1)
                turned(n + 1)
                if isinstance(n, int) and n == SH - 2:
                    dve.wait_ge(index_ready, 16)
                pick(n + 2)
                dve.wait_ge(h_turned, n + 1)
                nc.vector.tensor_copy(hT[:], h_ps[:, 0:F].rearrange("p (k t) -> p k t", k=F // P)).then_inc(h_copied, 1)
                dve.wait_ge(downed, n * 2 + 2)
                wait(dve, y_out, n * 16)
                nc.vector.tensor_copy(y[:, 512:D], y_ps[1][:]).then_inc(y_dve, 1)
            blocks(dve, body)


def combine(nc, g):
    with ExitStack() as ctx:
        sb = lambda n, s, dt=F32: ctx.enter_context(nc.sbuf_tensor(n, s, dt))
        ln_g, ln_b = sb("ln2_g", [P, D]), sb("ln2_b", [P, D])
        row = [[sb(f"y_row{u}_{k}", [P, D]) for k in range(TOPK)] for u in range(2)]
        res, acc = [sb(f"x1_row{u}", [P, D]) for u in range(2)], [sb(f"y_shared{u}", [P, D]) for u in range(2)]
        out = [sb(f"y_tile{u}", [P, D]) for u in range(2)]
        st, mv, rs, eps = sb("l2_stats", [P, 2, 6]), sb("l2_meanvar", [P, 2]), sb("l2_rstd", [P, 2]), sb("eps2", [P, 1])
        w_in, eps_ready, rows0, rows1, tile0, tile1, step, root, out0, out1 = sems(
            nc, ctx, "p6_w_in", "eps2_ready", "rows_in0", "rows_in1", "tile_in0", "tile_in1", "comb_step", "comb_root",
            "y_out0", "y_out1")
        rows_in, tile_in, stored = (rows0, rows1), (tile0, tile1), (out0, out1)
        STEPS = TOPK + 7
        block = ctx.enter_context(nc.Block())

        def tiles(eng, body):
            def pair(i):
                for u in range(2):
                    body(i, u, P)
            loop(eng, QT // 2, pair)
            body(QT // 2, 0, TAIL)

        @block.sync
        def _(sp):
            sp.dma_start(ln_g[:], g.ln2_g[0].partition_broadcast(P)).then_inc(w_in, 16)
            sp.dma_start(ln_b[:], g.ln2_b[0].partition_broadcast(P)).then_inc(w_in, 16)

            def read(i, u, n):
                wait(sp, step, (2 * i + (u - 2)) * STEPS + TOPK + 1)
                at = ds(i * (2 * P) + u * P, n)
                sp.dma_start(res[u][0:n, :], g.x1[at, :]).then_inc(tile_in[u], 16)
                wait(sp, step, (2 * i + (u - 1)) * STEPS)
                sp.dma_start(acc[u][0:n, :], g.y[at, :]).then_inc(tile_in[u], 16)

            def write(i, u, n):
                sp.wait_ge(step, (2 * i + (u + 1)) * STEPS)
                to = g.y_sample if n == TAIL else g.y_prompt[ds(i * (2 * P) + u * P, P), :]
                sp.dma_start(to, out[u][0:n, :]).then_inc(stored[u], 16)
            read(0, 0, P)

            def body(i):
                for u in range(2):
                    if u == 0:
                        read(i, 1, P)
                    else:
                        read(i + 1, 0, P)
                    write(i, u, P)
            loop(sp, QT // 2 - 1, body)
            read(QT // 2 - 1, 1, P)
            write(QT // 2 - 1, 0, P)
            read(QT // 2, 0, TAIL)
            write(QT // 2 - 1, 1, P)
            write(QT // 2, 0, TAIL)
            sp.wait_ge(stored[0], 16 * (QT // 2 + 1))
            sp.wait_ge(stored[1], 16 * (QT // 2))

        @block.gpsimd
        def _(pool):
            for t in range(TT):
                u, n = t % 2, P if t < QT else TAIL
                for k in range(TOPK):
                    wait(pool, step, (t - 2) * STEPS + k + 1)
                    pool.indirect_dma_start(out=row[u][k][0:n, :], out_offset=None, in_=g.y,
                                            in_offset=bass.IndirectOffsetOnAxis(
                                                ap=g.row8[:].bitcast(U32)[0:n, t, k:k + 1], axis=0)
                                            ).then_inc(rows_in[u], 16)

        @block.scalar
        def _(act):
            act.wait_ge(eps_ready, 1)

            def body(i, u, n):
                act.wait_ge(step, (2 * i + u) * STEPS + TOPK + 3)
                nc.scalar.activation(rs[0:n, 0:1], mv[0:n, 1:2], ACT.Sqrt, bias=eps[0:n, :]).then_inc(root, 1)
            tiles(act, body)

        @block.vector
        def _(dve):
            nc.vector.memset(eps[:], EPS).then_inc(eps_ready, 1)
            dve.wait_ge(w_in, 32)

            def body(i, u, n):
                b = (2 * i + u) * STEPS
                a = acc[u][0:n, :]
                dve.wait_ge(tile_in[u], i * 32 + 32)
                dve.wait_ge(rows_in[u], i * (16 * TOPK) + 16 * TOPK)
                for k in range(TOPK):
                    nc.vector.scalar_tensor_tensor(
                        out=a, in0=row[u][k][0:n, :], scalar=g.weight8[0:n, ds(i * 2 + u, 1), k:k + 1].rearrange(
                            "p a b -> p (a b)"), in1=a, op0=ALU.mult, op1=ALU.add).then_inc(step, 1)
                    dve.wait_ge(step, b + (k + 1))
                nc.vector.scalar_tensor_tensor(out=a, in0=res[u][0:n, :], scalar=ALPHA, in1=a, op0=ALU.mult,
                                               op1=ALU.add).then_inc(step, 1)
                dve.wait_ge(step, b + (TOPK + 1))
                for half in range(2):
                    ins = nc.vector.bn_stats(st[0:n, half, :], acc[u][0:n, half * 512:(half + 1) * 512])
                ins.then_inc(step, 1)
                held(dve, step, b + (TOPK + 2), g.passed)
                nc.vector.bn_aggr(mv[0:n, :], st[0:n].rearrange("p a b -> p (a b)")).then_inc(step, 1)
                dve.wait_ge(root, i * 2 + (u + 1))
                nc.vector.reciprocal(rs[0:n, 1:2], rs[0:n, 0:1]).then_inc(step, 1)
                dve.wait_ge(step, b + (TOPK + 4))
                nc.vector.tensor_scalar(a, a, mv[0:n, 0:1], rs[0:n, 1:2], ALU.subtract, ALU.mult).then_inc(step, 1)
                dve.wait_ge(step, b + (TOPK + 5))
                nc.vector.tensor_tensor(a, a, ln_g[0:n, :], ALU.mult).then_inc(step, 1)
                dve.wait_ge(step, b + (TOPK + 6))
                wait(dve, stored[u], i * 16)
                nc.vector.tensor_tensor(out[u][0:n, :], a, ln_b[0:n, :], ALU.add).then_inc(step, 1)
            tiles(dve, body)


PHASES = [constants, mixing_weight, in_projection, prompt_attention, decode_attention, mix_and_route, plan_dispatch, experts, combine]

class Tensors:
    pass


def build(nc, inputs, outputs):
    g = Tensors()
    (g.x_prompt, g.x_sample, g.cache_k, g.cache_v, g.state_conv, g.page_table, g.w_in, g.lam_q1, g.lam_k1, g.lam_q2,
     g.lam_k2, g.subln_g, g.w_dw, g.b_dw, g.conv_ln_g, g.conv_ln_b, g.w_o, g.ln1_g, g.ln1_b, g.w_router, g.b_router,
     g.w_gate, g.w_up, g.w_down, g.w_sh_gate, g.w_sh_up, g.w_sh_down, g.ln2_g, g.ln2_b) = inputs
    (g.y_prompt, g.y_sample, g.k_prompt, g.v_prompt, g.conv_prompt, g.k_sample, g.v_sample, g.conv_sample) = outputs
    g.x_prompt = g.x_prompt.rearrange("b s d -> (b s) d")
    g.x_sample = g.x_sample.rearrange("b s d -> (b s) d")
    g.y_prompt = g.y_prompt.rearrange("b s d -> (b s) d")
    g.y_sample = g.y_sample.rearrange("b s d -> (b s) d")
    g.w_in = g.w_in.rearrange("l d e -> (l d) e")
    g.k_prompt, g.v_prompt, g.k_sample, g.v_sample = (
        t.rearrange("l b s h d -> (l b s) (h d)") for t in (g.k_prompt, g.v_prompt, g.k_sample, g.v_sample))
    scratch = lambda n, s, dt=F32: nc.dram_tensor(n, s, dt, kind="Internal").ap()
    g.x_tail = scratch("x_tail", [P, D])
    g.qT = scratch("qT_s", [H, P, TP])
    g.kT = scratch("kT_s", [H, P, TP])
    g.convT = scratch("convT_s", [H, P, TP])
    g.conv_prompt = g.conv_prompt.rearrange("l b r c -> (l b r) c")
    g.conv_sample = g.conv_sample[0]
    g.attn = scratch("attn_s", [TP, C])
    g.x1 = scratch("x1_s", [TP, D])
    g.y = scratch("y_s", [NBLK * P, D])
    g.slot_token = scratch("slot_token", [P * NBLK], U32)
    with ExitStack() as ctx:
        g.passed, = sems(nc, ctx, "passed")
        sb = lambda n, s, dt=F32: ctx.enter_context(nc.sbuf_tensor(n, s, dt))
        g.ident = sb("ident", [P, P])
        g.ident_bf = sb("ident_bf", [P, P], BF16)
        g.causal = sb("causal", [P, P], BF16)
        g.neg_lam = sb("neg_lam", [P, 1])
        g.valid = sb("valid", [P, TT])
        g.iota_e = sb("iota_e", [P, 8])
        g.chosen = sb("chosen", [P, TT, E])
        g.weight = sb("weight", [P, TT, E])
        g.weight8 = sb("weight8", [P, TT, TOPK])
        g.row8 = sb("row8", [P, TT, TOPK], I32)
        g.place8 = sb("place8", [P, TT, TOPK], U32)
        g.bounds = sb("bounds", [1, E + 2], I32)
        for phase in PHASES:
            phase(nc, g)


_INS = ["x_prompt", "x_sample", "cache_k", "cache_v", "state_conv", "page_table", "w_in", "lam_q1", "lam_k1",
        "lam_q2", "lam_k2", "subln_g", "w_dw", "b_dw", "conv_ln_g", "conv_ln_b", "w_o", "ln1_g", "ln1_b", "w_router",
        "b_router", "w_gate", "w_up", "w_down", "w_sh_gate", "w_sh_up", "w_sh_down", "ln2_g", "ln2_b"]
_OUTS = [(1, SEQ, D), (NSEQ, NEW, D), (1, 1, SEQ, H, P), (1, 1, SEQ, H, P), (1, 1, 30, C),
         (1, NSEQ, NEW, H, P), (1, NSEQ, NEW, H, P), (1, NSEQ, 30, C)]


def kernel(**inputs):
    import numpy as _np
    import concourse.bacc as _bacc
    from concourse import mybir as _mybir
    from concourse.bass_utils import run_bass_kernel_spmd as _run

    nc = _bacc.Bacc("TRN2", target_bir_lowering=False, num_devices=1)
    arrays, ins, outs = {}, [], []
    for name in _INS:
        a = _np.ascontiguousarray(inputs[name])
        arrays[f"in_{name}_dram"] = a
        ins.append(nc.dram_tensor(f"in_{name}_dram", a.shape, _mybir.dt.from_np(a.dtype), kind="ExternalInput").ap())
    for i, shape in enumerate(_OUTS):
        outs.append(nc.dram_tensor(f"out_{i}_dram", shape, _mybir.dt.float32, kind="ExternalOutput").ap())
    build(nc, ins, outs)
    r = _run(nc, [arrays], core_ids=[0])
    return tuple(r.results[0][f"out_{i}_dram"] for i in range(len(_OUTS)))
```

```python
from contextlib import ExitStack

import concourse.bass as bass
import concourse.mybir as mybir

ALU = mybir.AluOpType
ACT = mybir.ActivationFunctionType
AX = mybir.AxisListType
F32 = mybir.dt.float32
BF16 = mybir.dt.bfloat16
F32R = mybir.dt.float32r
I32 = mybir.dt.int32
U32 = mybir.dt.uint32
ds = bass.ds

P = 128
D = 1024
KT = D // P
SEQ = 2048
QT = SEQ // P
NSEQ = 8
NEW = 8
TOK = SEQ + NSEQ * NEW
TT = -(-TOK // P)
TP = TT * P
TAIL = TOK - QT * P
H = 4
HD = 64
C = 512
IN_W = 5 * C
CHUNKS = [(c * 512, 512) for c in range(SEQ // 512)] + [(SEQ, P)]
NEG = -1.0e30
LAMBDA_INIT = 0.2
EPS = 1e-5


def sems(nc, ctx, *names):
    return [ctx.enter_context(nc.semaphore(n)) for n in names]


def wait(eng, sem, count):
    if not isinstance(count, int) or count > 0:
        eng.wait_ge(sem, count)


def held(eng, sem, count, passed):
    wait(eng, sem, count)
    eng.sem_inc(passed, 1)


def loop(eng, n, body):
    body(0)
    if n > 1:
        with eng.Fori(1, n) as i:
            body(i)


def constants(nc, g):
    with ExitStack() as ctx:
        zeroed, = sems(nc, ctx, "const_zeroed")
        valid_made, = sems(nc, ctx, "valid_made")
        block = ctx.enter_context(nc.Block())

        @block.gpsimd
        def _(pool):
            nc.gpsimd.memset(g.ident[:], 0.0)
            nc.gpsimd.memset(g.ident_bf[:], 0.0)
            nc.gpsimd.memset(g.causal[:], 0.0).then_inc(zeroed, 1)
            nc.gpsimd.memset(g.valid[:], 1.0).then_inc(valid_made, 1)
            nc.gpsimd.iota(g.iota_e[:], pattern=[[1, 8]], base=0, channel_multiplier=0,
                           allow_small_or_imprecise_dtypes=True)
            pool.wait_ge(zeroed, 1)
            pool.wait_ge(valid_made, 1)
            nc.gpsimd.affine_select(out=g.valid[:, QT:TT], in_=g.valid[:, QT:TT], compare_op=ALU.is_ge, fill=0.0,
                                    base=TAIL - 1, pattern=[[0, 1]], channel_multiplier=-1)
            for m in (g.ident, g.ident_bf):
                nc.gpsimd.affine_select(out=m[:], in_=m[:], compare_op=ALU.not_equal, fill=1.0, base=0,
                                        pattern=[[-1, P]], channel_multiplier=1)
            nc.gpsimd.affine_select(out=g.causal[:], in_=g.causal[:], compare_op=ALU.is_ge, fill=NEG, base=0,
                                    pattern=[[-1, P]], channel_multiplier=1)


TAPS = 31
PAST = TAPS - 1
EXT = PAST + NEW
UW = PAST + SEQ + NSEQ * EXT


def in_projection(nc, g):
    with ExitStack() as ctx:
        sb = lambda n, s, dt=F32: ctx.enter_context(nc.sbuf_tensor(n, s, dt))
        xT = sb("xT", [P, KT, TP])
        xin = [sb(f"xin{u}", [P, D]) for u in range(2)]
        wcol = [sb(f"wcol{u}", [P, KT, P]) for u in range(2)]
        feat = [sb(f"feat{u}", [P, TP]) for u in range(2)]
        rows = [sb(f"rows{u}", [P, TT, P]) for u in range(2)]
        units = [sb(f"glu{i}", [P, UW]) for i in range(H)]
        gate = sb("glu_gate", [P, TP])
        conv = sb("conv_sum", [P, TP])
        fresh = sb("glu_fresh", [P, H, TAIL])
        state = feat[0][:, 0:2 * C].rearrange("p (g c) -> p g c", g=2)
        taps_in = rows[0][0:TAPS, 0:H, :]
        taps = sb("conv_taps", [P, H, TAPS])
        bias = sb("conv_bias", [P, H])
        last_p = rows[1][0:PAST, 0:H, :]
        last_s = rows[1][0:TAIL, H:2 * H, :]
        bank = [ctx.enter_context(nc.psum_tensor(f"p1_bank{b}", [P, 512], F32)) for b in range(8)]
        (small_in, state_turned, state_kept, zeroed, x_in0, x_in1, x_zeroed, xt_ready, xt_act, xt_dve, w_in0, w_in1,
         acc_ready, feat_ready, glu_ready, last_turned, last_kept, last_out, conv_step, conv_out, stored0,
         stored1, rows_ps, rows_ready, rows_out0, rows_out1, tail_out) = sems(
            nc, ctx, "small_in", "state_turned", "state_kept", "units_zeroed", "x_in0", "x_in1", "x_zeroed",
            "xt_ready", "xt_act", "xt_dve", "w_in0", "w_in1", "acc_ready", "feat_ready", "glu_ready", "last_turned",
            "last_kept", "last_out", "conv_step", "conv_out", "feat_stored0", "feat_stored1", "rows_ps",
            "rows_ready", "rows_out0", "rows_out1", "tail_out")
        x_in, w_arrived = (x_in0, x_in1), (w_in0, w_in1)
        feat_stored, rows_out = (stored0, stored1), (rows_out0, rows_out1)
        w_v = g.w_in.rearrange("(k p) n -> p k n", p=P)
        NCH = len(CHUNKS)
        QF, KF, VF = 2 * H, 3 * H, 4 * H
        sample = lambda i, a, b: units[i][:, PAST + SEQ:].rearrange("p (b r) -> p b r", r=EXT)[:, :, a:b]
        block = ctx.enter_context(nc.Block())

        @block.sync
        def _(sp):
            for half in range(2):
                sp.dma_start(state[0:4 * PAST, half, :], g.state_conv[0, 4 * half:4 * half + 4, :, :]
                             .rearrange("b r c -> (b r) c")).then_inc(small_in, 16)
            sp.dma_start(taps_in, g.w_dw[0].rearrange("j (i p) -> j i p", p=P)).then_inc(small_in, 16)
            with nc.allow_non_contiguous_dma("512 biases, one per channel"):
                sp.dma_start(bias[:], g.b_dw[0].rearrange("(i p) -> p i", p=P)).then_inc(small_in, 16)

            def load_x(i):
                for u in range(2):
                    wait(sp, xt_ready, (2 * i + u - 1) * 2)
                    sp.dma_start(xin[u][:], g.x_prompt[ds(i * 2 * P + u * P, P), :]).then_inc(x_in[u], 16)
            loop(sp, QT // 2, load_x)
            sp.wait_ge(x_zeroed, 1)
            sp.dma_start(xin[0][0:TAIL, :], g.x_sample).then_inc(x_in[0], 16)
            sp.wait_ge(x_in[0], 16 * (QT // 2 + 1))
            sp.dma_start(g.x_tail, xin[0][:]).then_inc(tail_out, 16)

            def load_w(first, column, i):
                for u in range(2):
                    wait(sp, acc_ready, (first + 2 * i + u - 1) * NCH)
                    sp.dma_start(wcol[u][:], w_v[:, :, ds(column(i, u), P)]).then_inc(w_arrived[u], 16)
            loop(sp, H, lambda i: load_w(0, lambda i, u: i * P + (4 * C - u * C), i))
            with sp.Fori(0, 3 * H // 2) as i:
                load_w(QF, lambda i, u: i * 2 * P + u * P, i)
            sp.wait_ge(tail_out, 16)

        @block.tensor
        def _(pe):
            pe.wait_ge(small_in, 64)
            for i in range(H):
                mm = nc.tensor.transpose(bank[4][:, i * 32:i * 32 + TAPS], taps_in[:, i, :], g.ident[0:TAPS, 0:TAPS])
            mm.then_inc(state_turned, 1)
            for half in range(2):
                for i in range(H):
                    mm = nc.tensor.transpose(bank[5 + half][:, i * P:i * P + 4 * PAST],
                                             state[0:4 * PAST, half, i * P:(i + 1) * P],
                                             g.ident[0:4 * PAST, 0:4 * PAST])
                mm.then_inc(state_turned, 1)

            def turn_x(u, tile, loaded):
                pe.wait_ge(x_in[u], loaded)
                for half, copied in ((0, xt_act), (1, xt_dve)):
                    wait(pe, copied, tile - 1)
                    for k in range(4):
                        mm = nc.tensor.transpose(bank[2 * u + half][:, k * P:(k + 1) * P],
                                                 xin[u][:, (4 * half + k) * P:(4 * half + k + 1) * P], g.ident[:])
                    mm.then_inc(xt_ready, 1)

            def turn_pair(i):
                for u in range(2):
                    turn_x(u, 2 * i + u, 16 * i + 16)
            loop(pe, QT // 2, turn_pair)
            turn_x(0, QT, 16 * (QT // 2 + 1))

            def products(u, c):
                s, n = CHUNKS[c]
                for k in range(KT):
                    mm = nc.tensor.matmul(bank[c][:, 0:n], wcol[u][:, k, :], xT[:, k, s:s + n],
                                          start=(k == 0), stop=(k == KT - 1))
                mm.then_inc(acc_ready, 1)

            def turn_rows(i, u, c):
                pe.wait_ge(feat_ready, (2 * i + (KF + u)) * NCH + (c + 1))
                wait(pe, rows_ready, (2 * i + u) * NCH + (c - 1))
                s, n = CHUNKS[c]
                for t in range(n // P):
                    mm = nc.tensor.transpose(bank[5 + (u * NCH + c) % 2][:, t * P:(t + 1) * P],
                                             feat[u][:, s + t * P:s + (t + 1) * P], g.ident[:])
                mm.then_inc(rows_ps, 1)

            def features(first, rows_too, i):
                for u in range(2):
                    pe.wait_ge(w_arrived[u], 16 * i + 16 * (first // 2 + 1))
                    for c in range(NCH):
                        wait(pe, feat_ready, (2 * i + (first + u - 1)) * NCH + (c + 1))
                        products(u, c)
                        if rows_too and c:
                            turn_rows(i, u, c - 1)
                    if rows_too:
                        turn_rows(i, u, NCH - 1)
            pe.wait_ge(xt_act, TT)
            pe.wait_ge(xt_dve, TT)
            pe.wait_ge(state_kept, 3)
            loop(pe, H, lambda i: features(0, False, i))
            with pe.Fori(0, H // 2) as i:
                features(QF, False, i)
            pe.wait_ge(glu_ready, H)
            for i in range(H):
                nc.tensor.transpose(bank[5][0:PAST, i * P:(i + 1) * P], units[i][:, SEQ:SEQ + PAST], g.ident[:])
                mm = nc.tensor.transpose(bank[6][0:TAIL, i * P:(i + 1) * P], fresh[:, i, :], g.ident[:])
            mm.then_inc(last_turned, 1)
            pe.wait_ge(last_kept, 2)
            loop(pe, H, lambda i: features(KF, True, i))

        @block.scalar
        def _(act):
            def keep_x(u, tile, column):
                act.wait_ge(xt_ready, 2 * tile + 1)
                nc.scalar.copy(xT[:, 0:4, ds(column, P)],
                               bank[2 * u][:].rearrange("p (k t) -> p k t", k=4)).then_inc(xt_act, 1)

            def keep_pair(i):
                for u in range(2):
                    keep_x(u, 2 * i + u, i * (2 * P) + u * P)
            loop(act, QT // 2, keep_pair)
            keep_x(0, QT, SEQ)

            for i in range(H):
                if i:
                    act.wait_ge(glu_ready, i)
                for c, (s, n) in enumerate(CHUNKS):
                    act.wait_ge(acc_ready, 2 * i * NCH + c + 1)
                    nc.scalar.activation(gate[:, s:s + n], bank[c][:, 0:n], ACT.Sigmoid).then_inc(feat_ready, 1)
                for c, (s, n) in enumerate(CHUNKS):
                    act.wait_ge(acc_ready, (2 * i + 1) * NCH + c + 1)
                    if s < SEQ:
                        nc.scalar.copy(units[i][:, PAST + s:PAST + s + n], bank[c][:, 0:n]).then_inc(feat_ready, 1)
                    else:
                        nc.scalar.copy(sample(i, PAST, EXT), bank[c][:, 0:TAIL].rearrange("p (b r) -> p b r", r=NEW)
                                       ).then_inc(feat_ready, 1)

            def keep_rows(i, u, c):
                act.wait_ge(rows_ps, (2 * i + u) * NCH + (c + 1))
                s, n = CHUNKS[c]
                nc.scalar.copy(rows[u][:, s // P:(s + n) // P, :],
                               bank[5 + (u * NCH + c) % 2][:, 0:n].rearrange("p (t f) -> p t f", f=P)
                               ).then_inc(rows_ready, 1)

            def keep_features(i, first, stored, kv):
                for u in range(2):
                    wait(act, feat_stored[u], stored)
                    if kv is not None:
                        wait(act, rows_ps, (kv + u - 1) * NCH)
                        wait(act, rows_out[u], 16 * kv)
                    for c, (s, n) in enumerate(CHUNKS):
                        act.wait_ge(acc_ready, (2 * i + (first + u)) * NCH + (c + 1))
                        nc.scalar.copy(feat[u][:, s:s + n], bank[c][:, 0:n]).then_inc(feat_ready, 1)
                        if kv is not None and c:
                            keep_rows(kv // 2, u, c - 1)
                    if kv is not None:
                        keep_rows(kv // 2, u, NCH - 1)
            act.wait_ge(state_turned, 3)
            loop(act, H // 2, lambda i: keep_features(i, QF, 16 * i, None))
            act.wait_ge(last_turned, 1)
            nc.scalar.copy(last_p, bank[5][0:PAST, :].rearrange("p (i c) -> p i c", c=P)).then_inc(last_kept, 1)
            nc.scalar.copy(last_s, bank[6][0:TAIL, :].rearrange("p (i c) -> p i c", c=P)).then_inc(last_kept, 1)
            act.wait_ge(last_out, 16 * (NSEQ + 2))
            keep_features(0, KF, 16 * (H // 2), 0)
            keep_features(1, KF, 16 * (H // 2 + 1), 2)
            keep_features(0, VF, 16 * H, H)
            keep_features(1, VF, 16 * H, H + 2)

        @block.vector
        def _(dve):
            for i in range(H):
                nc.vector.memset(units[i][:, 0:PAST], 0.0).then_inc(zeroed, 1)
            nc.vector.memset(conv[:, TOK:TP], 0.0).then_inc(zeroed, 1)
            dve.wait_ge(state_turned, 1)
            nc.vector.tensor_copy(taps[:], bank[4][:, 0:32 * H].rearrange("p (i j) -> p i j", j=32)[:, :, 0:TAPS]
                                  ).then_inc(state_kept, 1)
            for half in range(2):
                dve.wait_ge(state_turned, 2 + half)
                for i in range(H):
                    ins = nc.vector.tensor_copy(
                        sample(i, 0, PAST)[:, 4 * half:4 * half + 4, :],
                        bank[5 + half][:, i * P:i * P + 4 * PAST].rearrange("p (b r) -> p b r", r=PAST))
                ins.then_inc(state_kept, 1)

            def keep_x(u, tile, column):
                dve.wait_ge(xt_ready, 2 * tile + 2)
                nc.vector.tensor_copy(xT[:, 4:8, ds(column, P)],
                                      bank[2 * u + 1][:].rearrange("p (k t) -> p k t", k=4)).then_inc(xt_dve, 1)

            def keep_pair(i):
                for u in range(2):
                    keep_x(u, 2 * i + u, i * (2 * P) + u * P)
            loop(dve, QT // 2, keep_pair)
            dve.wait_ge(xt_ready, 2 * (QT - 1))
            nc.vector.memset(xin[0][:], 0.0).then_inc(x_zeroed, 1)
            keep_x(0, QT, SEQ)

            dve.wait_ge(zeroed, H + 1)
            dve.wait_ge(state_kept, 3)
            step = 0
            for i in range(H):
                dve.wait_ge(glu_ready, i + 1)
                if i:
                    dve.wait_ge(conv_out, 16 * i)
                for j in range(TAPS):
                    for what in range(2):
                        if j:
                            dve.wait_ge(conv_step, step - 1)
                        if what == 0:
                            src, acc = units[i][:, j:j + SEQ], conv[:, 0:SEQ]
                        else:
                            src = sample(i, j, j + NEW)
                            acc = conv[:, SEQ:TOK].rearrange("p (b r) -> p b r", r=NEW)
                        if j == 0:
                            nc.vector.tensor_scalar(acc, src, taps[:, i, 0:1], bias[:, i:i + 1], ALU.mult, ALU.add
                                                    ).then_inc(conv_step, 1)
                        else:
                            nc.vector.scalar_tensor_tensor(out=acc, in0=src, scalar=taps[:, i, j:j + 1], in1=acc,
                                                           op0=ALU.mult, op1=ALU.add).then_inc(conv_step, 1)
                        step += 1

        @block.gpsimd
        def _(pool):
            pool.dma_start(g.conv_sample[:, 0:PAST - NEW, :], g.state_conv[0, :, NEW:PAST, :]).then_inc(last_out, 16)
            for i in range(H):
                pool.wait_ge(feat_ready, 2 * (i + 1) * NCH)
                u = units[i][:, PAST:PAST + SEQ]
                nc.gpsimd.tensor_tensor(u, u, gate[:, 0:SEQ], ALU.mult)
                nc.gpsimd.tensor_tensor(fresh[:, i, :].rearrange("p (b r) -> p b r", r=NEW), sample(i, PAST, EXT),
                                        gate[:, SEQ:TOK].rearrange("p (b r) -> p b r", r=NEW), ALU.mult)
                nc.gpsimd.tensor_tensor(sample(i, PAST, EXT), sample(i, PAST, EXT),
                                        gate[:, SEQ:TOK].rearrange("p (b r) -> p b r", r=NEW), ALU.mult
                                        ).then_inc(glu_ready, 1)
            CONV_STEPS = 2 * TAPS

            def store_conv(i):
                pool.wait_ge(conv_step, CONV_STEPS * (i + 1))
                pool.dma_start(g.convT[i], conv[:]).then_inc(conv_out, 16)

            def store_feature(i, first, to):
                for u in range(2):
                    pool.wait_ge(feat_ready, (2 * i + first + u + 1) * NCH)
                    pool.dma_start(to[2 * i + u], feat[u][:]).then_inc(feat_stored[u], 16)

            def store_rows(i, at, to_prompt, to_sample):
                for u in range(2):
                    pool.wait_ge(rows_ready, (2 * i + at + u + 1) * NCH)
                    h = (2 * i + u) * P
                    pool.dma_start(to_prompt.rearrange("(t p) f -> p t f", p=P)[:, :, h:h + P],
                                   rows[u][:, 0:QT, :]).then_inc(rows_out[u], 16)
                    pool.dma_start(to_sample[:, h:h + P], rows[u][0:TAIL, QT, :]).then_inc(rows_out[u], 16)

            store_feature(0, QF, g.qT)
            store_feature(1, QF, g.qT)
            pool.wait_ge(last_kept, 2)
            pool.dma_start(g.conv_prompt, last_p.rearrange("p i c -> p (i c)")).then_inc(last_out, 16)
            for b in range(NSEQ):
                pool.dma_start(g.conv_sample[b, PAST - NEW:PAST, :], last_s[NEW * b:NEW * (b + 1)]
                               .rearrange("p i c -> p (i c)")).then_inc(last_out, 16)
            store_conv(0)
            store_feature(0, KF, g.kT)
            store_rows(0, 0, g.k_prompt, g.k_sample)
            store_conv(1)
            store_feature(1, KF, g.kT)
            store_rows(1, 0, g.k_prompt, g.k_sample)
            store_conv(2)
            store_rows(0, H, g.v_prompt, g.v_sample)
            store_conv(3)
            store_rows(1, H, g.v_prompt, g.v_sample)
            pool.wait_ge(last_out, 16 * (NSEQ + 2))
            pool.wait_ge(conv_out, 16 * H)
            for u in range(2):
                pool.wait_ge(feat_stored[u], 16 * H)
                pool.wait_ge(rows_out[u], 32 * H)


SCALE = float(HD) ** -0.5


def mixing_weight(nc, g):
    with ExitStack() as ctx:
        vec = ctx.enter_context(nc.sbuf_tensor("lam_vectors", [P, 4, HD], F32))
        prod = ctx.enter_context(nc.sbuf_tensor("lam_products", [P, 2, HD], F32))
        dot = ctx.enter_context(nc.sbuf_tensor("lam_dots", [P, 2], F32))
        ex = ctx.enter_context(nc.sbuf_tensor("lam_exps", [P, 2], F32))
        vectors_in, dot_done, exp_done, made = sems(nc, ctx, "lam_in", "lam_dot", "lam_exp", "lam_made")
        block = ctx.enter_context(nc.Block())

        @block.sync
        def _(sp):
            for n, v in enumerate((g.lam_q1, g.lam_k1, g.lam_q2, g.lam_k2)):
                sp.dma_start(vec[:, n, :], v.partition_broadcast(P)).then_inc(vectors_in, 16)

        @block.vector
        def _(dve):
            dve.wait_ge(vectors_in, 64)
            for n in range(2):
                nc.vector.tensor_tensor_reduce(prod[:, n, :], vec[:, 2 * n, :], vec[:, 2 * n + 1, :], 1.0, 0.0,
                                               ALU.mult, ALU.add, dot[:, n:n + 1]).then_inc(dot_done, 1)
            dve.wait_ge(exp_done, 1)
            nc.vector.tensor_scalar(ex[:, 1:2], ex[:, 1:2], -LAMBDA_INIT, None, ALU.add).then_inc(made, 1)
            dve.wait_ge(made, 1)
            nc.vector.tensor_tensor(g.neg_lam[:], ex[:, 1:2], ex[:, 0:1], ALU.subtract).then_inc(made, 1)

        @block.scalar
        def _(act):
            act.wait_ge(dot_done, 2)
            nc.scalar.activation(ex[:], dot[:], ACT.Exp).then_inc(exp_done, 1)


def prompt_attention(nc, g):
    with ExitStack() as ctx:
        sb = lambda n, s, dt=F32: ctx.enter_context(nc.sbuf_tensor(n, s, dt))
        q = [sb(f"q_head{u}", [P, SEQ]) for u in range(2)]
        k = [sb(f"k_head{u}", [P, SEQ]) for u in range(2)]
        v = [sb(f"v_head{u}", [P, QT, P]) for u in range(2)]
        out = [sb(f"o_head{u}", [P, QT, P]) for u in range(2)]
        prob = [[sb(f"prob{m}_{b}", [P, SEQ]) for m in range(2)] for b in range(3)]
        turned = [sb(f"mix_turned{b}", [P, 512]) for b in range(2)]
        mx = sb("row_max_parts", [P, 3, 2, 4])
        top = sb("row_max", [P, 3, 2])
        bias = sb("exp_bias", [P, 3, 2])
        part = sb("row_sum_parts", [P, 3, 2, 4])
        total = sb("row_sums", [P, 3, 2])
        recip = sb("row_recips", [P, 3, 2])
        coef = sb("mix_coef", [P, 3])
        ring = [ctx.enter_context(nc.psum_tensor(f"scores{b}", [P, 512], F32)) for b in range(5)]
        turn = [ctx.enter_context(nc.psum_tensor(f"turn{b}", [P, 512], F32)) for b in range(2)]
        o_ps = ctx.enter_context(nc.psum_tensor("o_ps", [P, 512], F32))
        (in0, in1, scores_ready, part_max, row_max, bias_ready, exp_done, summed, inverted, coef_ready, mixed, ps_turned,
         sb_turned, pv_done, o_kept, out_free, out0, out1) = sems(
            nc, ctx, "head_in0", "head_in1", "scores_ready", "part_max", "row_max", "bias_ready", "exp_done", "summed",
            "inverted", "coef_ready", "mixed", "ps_turned", "sb_turned", "pv_done", "o_kept", "out_free",
            "out_stored0", "out_stored1")
        head_in, stored = (in0, in1), (out0, out1)
        NCH = [qi // 4 + 1 for qi in range(QT)]
        before = [sum(NCH[:qi]) for qi in range(QT + 1)]
        GH, SH = before[QT], 2 * before[QT]
        RING, TURNS = len(ring), len(turn)
        width = lambda qi, c: min(512, (qi + 1) * P - c * 512)
        chunk_no = lambda qi, m, c: 2 * before[qi] + m * NCH[qi] + c
        E_FREE = 1

        cut = lambda qi: (NCH[qi] + 2) // 2

        def steps():
            for qi in range(QT + 2):
                if qi < QT:
                    yield "scores", qi, 0
                if 1 <= qi <= QT:
                    yield "mix", qi - 1, None
                if qi >= 2:
                    yield "product", qi - 2, 0
                if qi < QT:
                    yield "scores", qi, 1
                if qi >= 2:
                    yield "product", qi - 2, 1

        def act_steps():
            for qi in range(QT + 2):
                for m in range(2):
                    if qi >= 2:
                        yield "product", qi - 2, m
                    if qi < QT:
                        yield "scores", qi, m

        block = ctx.enter_context(nc.Block())

        @block.sync
        def _(sp):
            def load(h):
                u = h % 2
                if h >= 2:
                    sp.wait_ge(pv_done, (h - 1) * GH + TURNS)
                sp.dma_start(q[u][:], g.qT[h, :, 0:SEQ]).then_inc(head_in[u], 16)
                sp.dma_start(k[u][:], g.kT[h, :, 0:SEQ]).then_inc(head_in[u], 16)
                sp.dma_start(v[u][:], g.v_prompt.rearrange("(t p) f -> p t f", p=P)[:, :, h * P:(h + 1) * P]
                             ).then_inc(head_in[u], 16)
            load(0)
            load(1)
            for h in range(H):
                u = h % 2
                sp.wait_ge(o_kept, (h + 1) * QT + 1)
                sp.dma_start(g.attn[0:SEQ, h * P:(h + 1) * P].rearrange("(t p) f -> p t f", p=P), out[u][:]
                             ).then_inc(stored[u], 16)
                if h + 2 < H:
                    load(h + 2)
                sp.wait_ge(stored[u], 16 * (h // 2 + 1))
                sp.sem_inc(out_free, 1)

        @block.tensor
        def _(pe):
            pe.sem_inc(ps_turned, E_FREE)
            pe.sem_inc(pv_done, TURNS)
            with pe.Fori(0, H // 2) as i:
                for u in range(2):
                    pe.wait_ge(head_in[u], 48 * i + 48)
                    for what, qi, m in steps():
                        if what == "scores":
                            for c in range(NCH[qi]):
                                n = chunk_no(qi, m, c)
                                b = ring[(u * SH + n) % RING]
                                pe.wait_ge(exp_done, i * (2 * SH) + (u * SH + n + 1))
                                w = width(qi, c)
                                last = c == NCH[qi] - 1
                                mm = nc.tensor.matmul(b[:, 0:w], q[u][m * HD:(m + 1) * HD, qi * P:(qi + 1) * P],
                                                      k[u][m * HD:(m + 1) * HD, c * 512:c * 512 + w],
                                                      start=True, stop=not last)
                                if last:
                                    mm = nc.tensor.matmul(b[:, w - P:w], g.ident_bf[:], g.causal[:],
                                                          start=False, stop=True)
                                mm.then_inc(scores_ready, 1)
                        elif what == "product":
                            if m == 0:
                                pe.wait_ge(mixed, i * (2 * QT) + (u * QT + qi + 1))
                            for c in (range(cut(qi)), range(cut(qi), NCH[qi] + 1))[m]:
                                if c < NCH[qi]:
                                    n = u * GH + before[qi] + c
                                    pe.wait_ge(sb_turned, i * (2 * GH) + (n + 1))
                                    for t in range(width(qi, c) // P):
                                        mm = nc.tensor.transpose(
                                            turn[n % TURNS][:, t * P:(t + 1) * P],
                                            prob[qi % 3][0][:, c * 512 + t * P:c * 512 + (t + 1) * P], g.ident[:])
                                    mm.then_inc(ps_turned, 1)
                                if c == 0:
                                    pe.wait_ge(o_kept, i * (2 * QT) + (u * QT + qi + 1))
                                    continue
                                n = u * GH + before[qi] + c - 1
                                pe.wait_ge(sb_turned, i * (2 * GH) + (n + 1 + TURNS))
                                for t in range(width(qi, c - 1) // P):
                                    key = 4 * (c - 1) + t
                                    mm = nc.tensor.matmul(o_ps[:, 0:P], turned[n % TURNS][:, t * P:(t + 1) * P],
                                                          v[u][:, key, :], start=(key == 0), stop=(key == qi))
                                mm.then_inc(pv_done, 1)

        @block.vector
        def _(dve):
            with dve.Fori(0, H // 2) as i:
                for u in range(2):
                    for what, qi, m in steps():
                        b = qi % 3
                        if what == "scores":
                            for c in range(NCH[qi]):
                                n = u * SH + chunk_no(qi, m, c)
                                dve.wait_ge(scores_ready, i * (2 * SH) + (n + 1))
                                nc.vector.tensor_reduce(mx[:, b, m, c:c + 1], ring[n % RING][:, 0:width(qi, c)],
                                                        AX.X, ALU.max).then_inc(part_max, 1)
                            dve.wait_ge(part_max, i * (2 * SH) + (n + 1))
                            nc.vector.tensor_reduce(top[:, b, m:m + 1], mx[:, b, m, 0:NCH[qi]], AX.X, ALU.max
                                                    ).then_inc(row_max, 1)
                            r = u * 2 * QT + 2 * qi + m + 1
                            dve.wait_ge(row_max, i * (4 * QT) + r)
                            nc.vector.tensor_scalar(bias[:, b, m:m + 1], top[:, b, m:m + 1], -SCALE, None, ALU.mult
                                                    ).then_inc(bias_ready, 1)
                        elif what == "mix":
                            r = u * QT + qi + 1
                            dve.wait_ge(exp_done, i * (2 * SH) + (RING + u * SH + 2 * before[qi + 1]))
                            nc.vector.tensor_reduce(total[:, b, :], part[:, b, :, 0:NCH[qi]], AX.X, ALU.add
                                                    ).then_inc(summed, 1)
                            dve.wait_ge(summed, i * (2 * QT) + r)
                            nc.vector.reciprocal(recip[:, b, :], total[:, b, :]).then_inc(inverted, 1)
                            dve.wait_ge(inverted, i * (2 * QT) + r)
                            nc.vector.scalar_tensor_tensor(out=coef[:, b:b + 1], in0=recip[:, b, 1:2],
                                                           scalar=total[:, b, 0:1], in1=g.neg_lam[:], op0=ALU.mult,
                                                           op1=ALU.mult).then_inc(coef_ready, 1)
                            dve.wait_ge(coef_ready, i * (2 * QT) + r)
                            w = (qi + 1) * P
                            nc.vector.scalar_tensor_tensor(out=prob[b][0][:, 0:w], in0=prob[b][1][:, 0:w],
                                                           scalar=coef[:, b:b + 1], in1=prob[b][0][:, 0:w],
                                                           op0=ALU.mult, op1=ALU.add).then_inc(mixed, 1)

        @block.scalar
        def _(act):
            act.sem_inc(exp_done, RING)
            act.sem_inc(sb_turned, TURNS)
            act.sem_inc(o_kept, 1)
            act.sem_inc(out_free, 2)
            with act.Fori(0, H // 2) as i:
                for u in range(2):
                    act.wait_ge(out_free, i * 2 + (u + 1))
                    for what, qi, m in act_steps():
                        b = qi % 3
                        if what == "scores":
                            act.wait_ge(bias_ready, i * (4 * QT) + (u * 2 * QT + 2 * qi + m + 1))
                            if m == 0:
                                last = before[qi - 2] if qi >= 3 else 0
                                act.wait_ge(ps_turned, i * (2 * GH) + (E_FREE + u * GH + last))
                            for c in range(NCH[qi]):
                                n = u * SH + chunk_no(qi, m, c)
                                w = width(qi, c)
                                nc.scalar.activation(prob[b][m][:, c * 512:c * 512 + w], ring[n % RING][:, 0:w],
                                                     ACT.Exp, bias=bias[:, b, m:m + 1], scale=SCALE,
                                                     accum_out=part[:, b, m, c:c + 1]).then_inc(exp_done, 1)
                        else:
                            for c in (range(min(cut(qi), NCH[qi])), range(cut(qi), NCH[qi]))[m]:
                                n = u * GH + before[qi] + c
                                w = width(qi, c)
                                act.wait_ge(ps_turned, i * (2 * GH) + (n + 1 + E_FREE))
                                act.wait_ge(pv_done, i * (2 * GH) + (n + 1))
                                nc.scalar.copy(turned[n % TURNS][:, 0:w], turn[n % TURNS][:, 0:w]
                                               ).then_inc(sb_turned, 1)
                            if m == 0:
                                continue
                            act.wait_ge(pv_done, i * (2 * GH) + (u * GH + before[qi + 1] + TURNS))
                            nc.scalar.activation(out[u][:, qi, :], o_ps[:, 0:P], ACT.Copy,
                                                 scale=recip[:, b, 0:1]).then_inc(o_kept, 1)


PAGES = 64
LOT = 4
LOTS = PAGES // LOT
RING = 4
LANES = P // LOT
KEYS = LOT * P
ROWS = 32
PIECES = LOTS + 1


def decode_attention(nc, g):
    with ExitStack() as ctx:
        sb = lambda n, s, dt=F32: ctx.enter_context(nc.sbuf_tensor(n, s, dt))
        table = sb("page_rows", [P, NSEQ * PAGES], I32)
        number, part_mod = sb("partition_no", [P, 2], I32), sb("partition_mods", [P, 2])
        row = sb("cache_rows", [P, NSEQ * LOTS], U32)
        klot = [sb(f"k_lot{x}", [P, LOT, C]) for x in range(RING)]
        vlot = [sb(f"v_lot{x}", [P, LOT, C]) for x in range(RING)]
        kt = [sb(f"k_turned{n}", [P, H, KEYS]) for n in range(2)]
        qz = sb("q_by_map", [P, NSEQ, H, ROWS])
        qcur = [sb(f"q_current{u}", [P, H, ROWS]) for u in range(2)]
        knew, vnew = sb("k_new", [P, H, P]), sb("v_new", [P, C])
        ahead, mask = sb("keys_ahead", [P, NSEQ, P]), sb("new_mask", [P, NSEQ, P])
        score = [sb(f"seq_scores{u}", [P, PAGES * P + P]) for u in range(2)]
        pT = [sb(f"probs_turned{n}", [P, KEYS]) for n in range(2)]
        mx, top, bias = sb("max_parts", [P, 2, PIECES]), sb("max_row", [P, 2]), sb("max_bias", [P, 2])
        part, total, recip = sb("sum_parts", [P, 2, PIECES]), sb("sum_row", [P, 2]), sb("sum_recip", [P, 2])
        select = sb("map_select", [P, H, NEW])
        onorm = sb("o_normed", [P, P])
        osb = sb("o_rows", [H * NEW, NSEQ, P])
        opad = sb("o_pad", [P - TAIL, C])
        tr = [ctx.enter_context(nc.psum_tensor(f"k_ps{n}", [P, 512], F32)) for n in range(H)]
        s_ps = [ctx.enter_context(nc.psum_tensor(f"s_ps{n}", [P, 512], F32)) for n in range(2)]
        pt_ps = ctx.enter_context(nc.psum_tensor("pt_ps", [P, 512], F32))
        o_ps = ctx.enter_context(nc.psum_tensor("od_ps", [P, 512], F32))
        k_in = sems(nc, ctx, *[f"k_lot_in{x}" for x in range(RING)])
        v_in = sems(nc, ctx, *[f"v_lot_in{x}" for x in range(RING)])
        (table_in, number_ready, mod_step, row_ready, zeroed, ahead_ready, late_masked, mask_ready, new_in, q_ready,
         select_ready, k_turned, kt_dve, kt_act, scored, s_kept, new_kept, part_max, row_max, bias_ready, exp_done,
         p_turned, pt_kept, pv_done, summed, inverted, o_normed, selected, o_kept, o_stored) = sems(
            nc, ctx, "table_in", "number_ready", "mod_step", "row_ready", "dec_zeroed", "ahead_ready", "late_masked",
            "mask_ready", "new_in", "q_ready", "select_ready", "k_turned", "kt_dve", "kt_act", "scored", "s_kept",
            "new_kept", "dec_part_max", "dec_row_max", "dec_bias", "dec_exp", "p_turned", "pt_kept", "dec_pv",
            "dec_summed", "dec_inverted", "o_normed", "selected", "dec_o_kept", "dec_o_stored")
        NEW_DMAS = 16 * (2 * H + 2)
        cache_k = g.cache_k[0].rearrange("n (l k) h d -> (n l) (k h d)", k=LOT)
        cache_v = g.cache_v[0].rearrange("n (l k) h d -> (n l) (k h d)", k=LOT)
        block = ctx.enter_context(nc.Block())
        piece = lambda n: slice(PAGES * P, PAGES * P + P) if n == 0 else slice((n - 1) * KEYS, n * KEYS)
        bank = lambda u, n: s_ps[(u * PIECES + n) % 2]
        held_p = lambda u, n: pT[(u * PIECES + n) % 2]

        def steps(eng, body):
            body(0, 0, True, False)
            body(1, 1, True, True)
            with eng.Fori(1, NSEQ // 2) as i:
                for u in range(2):
                    body(i * 2 + u, u, True, True)
            body(NSEQ, 0, False, True)

        @block.sync
        def _(sp):
            sp.dma_start(table[:], g.page_table.rearrange("b n -> (b n)").partition_broadcast(P)).then_inc(table_in, 16)
            sp.wait_ge(zeroed, 3)
            for h in range(H):
                for m in range(2):
                    sp.dma_start(qz[m * HD:(m + 1) * HD, :, h, m * NEW:(m + 1) * NEW],
                                 g.qT[h, m * HD:(m + 1) * HD, SEQ:TOK].rearrange("p (b q) -> p b q", q=NEW)
                                 ).then_inc(new_in, 16)
            sp.dma_start(knew[:], g.kT.rearrange("h p t -> p h t")[:, :, SEQ:TP]).then_inc(new_in, 16)
            sp.dma_start(vnew[0:TAIL, :], g.v_sample).then_inc(new_in, 16)
            sp.dma_start(g.attn[TOK:TP, :], opad[:]).then_inc(o_stored, 16)
            sp.wait_ge(o_kept, NSEQ)
            for h in range(H):
                sp.dma_start(g.attn[SEQ:TOK, h * P:(h + 1) * P].rearrange("(b q) d -> q b d", q=NEW),
                             osb[h * NEW:(h + 1) * NEW, :, :]).then_inc(o_stored, 16)
            sp.wait_ge(o_stored, 16 * (H + 1))

        @block.tensor
        def _(pe):
            pe.wait_ge(new_in, NEW_DMAS)
            pe.wait_ge(select_ready, 1)

            def body(b, u, scores, products):
                def turn(l):
                    pe.wait_ge(k_in[l % RING], b * (16 * LOTS // RING) + 16 * (l // RING + 1))
                    for h in range(H):
                        wait(pe, (kt_dve, kt_act)[h % 2], b * (2 * LOTS) + (2 * (l - 1) + h // 2 + 1))
                        for a in range(LOT):
                            mm = nc.tensor.transpose(tr[h][:, a * P:(a + 1) * P],
                                                     klot[l % RING][:, a, h * P:(h + 1) * P], g.ident[:])
                        mm.then_inc(k_turned, 1)

                def score_new():
                    pe.wait_ge(q_ready, b + 1)
                    wait(pe, s_kept, b * LOTS - 1)
                    for h in range(H):
                        mm = nc.tensor.matmul(bank(u, 0)[h * ROWS:(h + 1) * ROWS, 0:P], qcur[u][:, h, :],
                                              knew[:, h, :], start=True, stop=True)
                    mm.then_inc(scored, 1)

                def score_lot(l):
                    pe.wait_ge(kt_dve, b * (2 * LOTS) + (2 * l + 2))
                    pe.wait_ge(kt_act, b * (2 * LOTS) + (2 * l + 2))
                    if l == 1:
                        pe.wait_ge(new_kept, b + 1)
                    else:
                        wait(pe, s_kept, b * LOTS + (l - 1 if l else 0))
                    for h in range(H):
                        mm = nc.tensor.matmul(bank(u, l + 1)[h * ROWS:(h + 1) * ROWS, :], qcur[u][:, h, :],
                                              kt[l % 2][:, h, :], start=True, stop=True)
                    mm.then_inc(scored, 1)

                def turn_probs(n):
                    pe.wait_ge(exp_done, b * PIECES + (n + 1 - PIECES))
                    wait(pe, pt_kept, b * PIECES + (n - PIECES))
                    at = piece(n)
                    for a in range((at.stop - at.start) // P):
                        mm = nc.tensor.transpose(pt_ps[:, a * P:(a + 1) * P],
                                                 score[1 - u][:, at.start + a * P:at.start + (a + 1) * P], g.ident[:])
                    mm.then_inc(p_turned, 1)

                def product(n):
                    pe.wait_ge(pt_kept, b * PIECES + (n + 1 - PIECES))
                    l = n - 1
                    if n == 0:
                        wait(pe, o_kept, b - 1)
                    else:
                        pe.wait_ge(v_in[l % RING], b * (16 * LOTS // RING) + (16 * (l // RING + 1) - 16 * LOTS // RING))
                    for a in range(LOT if n else 1):
                        for h in range(H):
                            v = vlot[l % RING][:, a, h * P:(h + 1) * P] if n else vnew[:, h * P:(h + 1) * P]
                            mm = nc.tensor.matmul(o_ps[h * ROWS:(h + 1) * ROWS, 0:P],
                                                  held_p(1 - u, n)[:, a * P + h * ROWS:a * P + (h + 1) * ROWS], v,
                                                  start=(n == 0), stop=(n == LOTS and a == LOT - 1))
                    mm.then_inc(pv_done, 1)

                if scores:
                    score_new()
                for n in range(LOTS + 3):
                    if scores and n < LOTS:
                        turn(n)
                    if scores and 1 <= n <= LOTS:
                        score_lot(n - 1)
                    if products and 1 <= n <= LOTS + 1:
                        turn_probs(n - 1)
                    if products and n >= 2:
                        product(n - 2)
                if products:
                    pe.wait_ge(o_normed, b)
                    nc.tensor.matmul(o_ps[0:H * NEW, P:2 * P], select[:].rearrange("p h q -> p (h q)"), onorm[:],
                                     start=True, stop=True).then_inc(selected, 1)
            steps(pe, body)

        @block.vector
        def _(dve):
            dve.wait_ge(number_ready, 1)
            for n, size in enumerate((LANES, NEW)):
                nc.vector.tensor_scalar(number[:, n:n + 1], number[:, n:n + 1], size - 1, None, ALU.bitwise_and
                                        ).then_inc(mod_step, 1)
            dve.wait_ge(mod_step, 2)
            nc.vector.tensor_copy(part_mod[:], number[:]).then_inc(mod_step, 1)
            dve.wait_ge(mod_step, 3)
            dve.wait_ge(ahead_ready, 1)
            a = ahead[:].rearrange("p b j -> p (b j)")
            nc.vector.tensor_scalar(a, a, part_mod[:, 1:2], 0.0, ALU.subtract, ALU.is_gt).then_inc(mod_step, 1)
            dve.wait_ge(mod_step, 4)
            nc.vector.tensor_scalar(mask[:].rearrange("p b j -> p (b j)"), a, NEG, None, ALU.mult
                                    ).then_inc(late_masked, 1)
            dve.wait_ge(table_in, 16)
            for a in range(LOT):
                at = slice(a * LANES, (a + 1) * LANES)
                nc.vector.tensor_scalar(row[at, :], table[at, :].rearrange("p (n a) -> p n a", a=LOT)[:, :, a],
                                        float(LANES), part_mod[at, 0:1], ALU.mult, ALU.add).then_inc(row_ready, 1)
            by_head = g.ident[:].rearrange("p (h r) -> p h r", r=ROWS)
            nc.vector.scalar_tensor_tensor(out=select[:], in0=by_head[:, :, NEW:2 * NEW], scalar=g.neg_lam[:],
                                           in1=by_head[:, :, 0:NEW], op0=ALU.mult, op1=ALU.add
                                           ).then_inc(select_ready, 1)
            dve.wait_ge(new_in, NEW_DMAS)
            dve.wait_ge(mask_ready, 1)

            def body(b, u, scores, products):
                def copy_keys(l):
                    for h in (0, 2):
                        dve.wait_ge(k_turned, b * (H * LOTS) + (l * H + h + 1))
                        wait(dve, scored, b * PIECES + l)
                        nc.vector.tensor_copy(kt[l % 2][:, h, :], tr[h][:]).then_inc(kt_dve, 1)

                def largest(n):
                    nc.vector.tensor_reduce(mx[:, u, n:n + 1], score[u][:, piece(n)], AX.X, ALU.max
                                            ).then_inc(part_max, 1)

                def keep_probs(n):
                    dve.wait_ge(p_turned, b * PIECES + (n + 1 - PIECES))
                    wait(dve, pv_done, b * PIECES + (n - 1 - PIECES))
                    w = KEYS if n else P
                    nc.vector.tensor_copy(held_p(1 - u, n)[:, 0:w], pt_ps[:, 0:w]).then_inc(pt_kept, 1)

                if scores:
                    nc.vector.tensor_copy(qcur[u][:], qz[:, ds(b, 1), :, :].rearrange("p a h r -> p (a h) r")
                                          ).then_inc(q_ready, 1)
                    dve.wait_ge(scored, b * PIECES + 1)
                    wait(dve, p_turned, b * PIECES - PIECES)
                    nc.vector.tensor_tensor(score[u][:, piece(0)], bank(u, 0)[:, 0:P],
                                            mask[:, ds(b, 1), :].rearrange("p a j -> p (a j)"), ALU.add
                                            ).then_inc(new_kept, 1)
                    dve.wait_ge(new_kept, b + 1)
                    largest(0)
                for n in range(LOTS + 2):
                    if scores and n < LOTS:
                        copy_keys(n)
                    if products and 1 <= n:
                        keep_probs(n - 1)
                    if scores and n >= 2:
                        dve.wait_ge(s_kept, b * LOTS + (n - 1))
                        largest(n - 1)
                if scores:
                    dve.wait_ge(part_max, (b + 1) * PIECES)
                    nc.vector.tensor_reduce(top[:, u:u + 1], mx[:, u, :], AX.X, ALU.max).then_inc(row_max, 1)
                    dve.wait_ge(row_max, b + 1)
                    nc.vector.tensor_scalar(bias[:, u:u + 1], top[:, u:u + 1], -SCALE, None, ALU.mult
                                            ).then_inc(bias_ready, 1)
                if products:
                    v = 1 - u
                    dve.wait_ge(exp_done, b * PIECES)
                    nc.vector.tensor_reduce(total[:, v:v + 1], part[:, v, :], AX.X, ALU.add).then_inc(summed, 1)
                    dve.wait_ge(summed, b)
                    nc.vector.reciprocal(recip[:, v:v + 1], total[:, v:v + 1]).then_inc(inverted, 1)
                    dve.wait_ge(inverted, b)
                    dve.wait_ge(pv_done, b * PIECES)
                    nc.vector.tensor_scalar(onorm[:], o_ps[:, 0:P], recip[:, v:v + 1], None, ALU.mult
                                            ).then_inc(o_normed, 1)
                    dve.wait_ge(selected, b)
                    nc.vector.tensor_copy(osb[:, ds(b - 1, 1), :].rearrange("p a d -> p (a d)"),
                                          o_ps[0:H * NEW, P:2 * P]).then_inc(o_kept, 1)
            steps(dve, body)

        @block.scalar
        def _(act):
            def body(b, u, scores, products):
                def copy_keys(l):
                    for h in (1, 3):
                        act.wait_ge(k_turned, b * (H * LOTS) + (l * H + h + 1))
                        wait(act, scored, b * PIECES + l)
                        nc.scalar.copy(kt[l % 2][:, h, :], tr[h][:]).then_inc(kt_act, 1)

                def keep_scores(l):
                    act.wait_ge(scored, b * PIECES + (l + 2))
                    if l == 0:
                        wait(act, p_turned, b * PIECES - PIECES)
                    nc.scalar.copy(score[u][:, piece(l + 1)], bank(u, l + 1)[:]).then_inc(s_kept, 1)

                def exponentials(n):
                    if n == 0:
                        act.wait_ge(bias_ready, b)
                        wait(act, summed, b - 2)
                    at = score[1 - u][:, piece(n)]
                    nc.scalar.activation(at, at, ACT.Exp, bias=bias[:, 1 - u:2 - u], scale=SCALE,
                                         accum_out=part[:, 1 - u, n:n + 1]).then_inc(exp_done, 1)

                for n in range(PIECES):
                    if scores and n < LOTS:
                        copy_keys(n)
                    if scores and n >= 1:
                        keep_scores(n - 1)
                    if products:
                        exponentials(n)
            steps(act, body)

        @block.gpsimd
        def _(pool):
            nc.gpsimd.iota(number[:], pattern=[[0, 2]], base=0, channel_multiplier=1).then_inc(number_ready, 1)
            nc.gpsimd.iota(ahead[:], pattern=[[-NEW, NSEQ], [1, P]], base=0, channel_multiplier=0,
                           allow_small_or_imprecise_dtypes=True).then_inc(ahead_ready, 1)
            for t in (qz, vnew, opad):
                nc.gpsimd.memset(t[:], 0.0).then_inc(zeroed, 1)
            pool.wait_ge(late_masked, 1)
            nc.gpsimd.affine_select(out=mask[:], in_=mask[:], compare_op=ALU.is_ge, fill=NEG, base=0,
                                    pattern=[[-NEW, NSEQ], [1, P]], channel_multiplier=0).then_inc(mask_ready, 1)

            def gather(to, arrived, cache, c, l):
                pool.indirect_dma_start(
                    out=to[l % RING][:].rearrange("p k c -> p (k c)"), out_offset=None, in_=cache,
                    in_offset=bass.IndirectOffsetOnAxis(ap=row[:, c * LOTS + l:c * LOTS + l + 1], axis=0)
                    ).then_inc(arrived[l % RING], 16)

            pool.wait_ge(row_ready, LOT)
            for b in range(NSEQ + 1):
                for l in range(LOTS):
                    if b < NSEQ:
                        wait(pool, k_turned, (b * LOTS + l + 1 - RING) * H)
                        gather(klot, k_in, cache_k, b, l)
                    if b:
                        wait(pool, pv_done, (b - 1) * PIECES + l + 2 - RING if l >= RING
                             else (b - 2) * PIECES + LOTS - RING + l + 2)
                        gather(vlot, v_in, cache_v, b - 1, l)
ALPHA = 2.0 ** 0.25
E = 64
EG = 8
TOPG = 4
TOPK = 8
ROUTED_SCALE = 2.5


def tile_pipeline(eng, body):
    body(-1, True, False, False)
    body(0, True, True, False)
    with eng.Fori(1, TT - 1) as t:
        body(t, True, True, True)
    body(TT - 1, False, True, True)
    body(TT, False, False, True)


def mix_and_route(nc, g):
    with ExitStack() as ctx:
        sb = lambda n, s, dt=F32: ctx.enter_context(nc.sbuf_tensor(n, s, dt))
        wo = sb("w_o", [P, KT, D])
        wr = sb("w_router", [P, KT, E])
        ln_g, ln_b = sb("ln1_g", [P, D]), sb("ln1_b", [P, D])
        cg, cb = sb("conv_g", [P, C]), sb("conv_b", [P, C])
        sub = sb("subln", [P, P])
        br = sb("b_router", [P, E])
        o_in, c_in, x_in = sb("o_in", [P, C]), sb("c_in", [P, H, P]), sb("x_res", [P, D])
        mix, mT = sb("mix", [P, D]), sb("mixT", [P, KT, P])
        res, x1, x1T = sb("residual", [P, D]), sb("x1", [P, D]), sb("x1T", [P, KT, P])
        square = sb("square", [P, C])
        rms, rstd = sb("rms", [P, H]), sb("rms_rstd", [P, H])
        cst, cmv, crs, cn = sb("c_stats", [P, 6]), sb("c_meanvar", [P, 2]), sb("c_rstd", [P, 2]), sb("c_norm", [P, C])
        lst, lmv, lrs = sb("l_stats", [P, 2, 6]), sb("l_meanvar", [P, 2]), sb("l_rstd", [P, 2])
        sig, sel, srt = sb("sigmoids", [P, E]), sb("selection", [P, E]), sb("group_sorted", [P, EG, 8])
        gs, g8, gi, gf = (sb("group_score", [P, EG]), sb("group_top", [P, 8]), sb("group_index", [P, 8], U32),
                          sb("group_index_f", [P, 8]))
        eq, gm, pen = sb("group_hits", [P, EG, TOPG]), sb("group_mask", [P, EG]), sb("group_penalty", [P, EG])
        v8, picked, hit = sb("top_values", [P, 8]), sb("picked", [P, E]), sb("hits", [P, E])
        w, ws, wrec = sb("raw_weights", [P, E]), sb("weight_sum", [P, 1]), sb("weight_recip", [P, 1])
        eps = sb("eps", [P, 1])
        bank = lambda n: ctx.enter_context(nc.psum_tensor(n, [P, 512], F32))
        c_ps, r_ps = bank("c_ps"), bank("router_ps")
        m_ps, p_ps, x_ps = ([bank(f"{n}{i}") for i in range(2)] for n in ("mix_ps", "proj_ps", "x1_ps"))
        (w_in, eps_ready, o_arr, c_arr, x_arr, c_turned, m_turned, m_copied, projected, x_turned, x_copied, routed,
         n_step, a_step, l_step, l_root, r_sig, r_step, x1_out) = sems(
            nc, ctx, "p4_w_in", "eps_ready", "o_arrived", "c_arrived", "x_arrived", "c_turned", "m_turned", "m_copied",
            "projected", "x1_turned", "x1_copied", "routed", "norm_step", "norm_act", "ln_step", "ln_root",
            "sig_ready", "route_step", "x1_out")
        block = ctx.enter_context(nc.Block())
        NS, AS, LS, RS = 10, 5, 8, 25

        @block.sync
        def _(sp):
            for dst, src in ((wo[:], g.w_o[0].rearrange("(k p) n -> p k n", p=P)),
                             (wr[:], g.w_router[0].rearrange("(k p) n -> p k n", p=P)),
                             (ln_g[:], g.ln1_g[0].partition_broadcast(P)), (ln_b[:], g.ln1_b[0].partition_broadcast(P)),
                             (cg[:], g.conv_ln_g[0].partition_broadcast(P)),
                             (cb[:], g.conv_ln_b[0].partition_broadcast(P)),
                             (sub[:], g.subln_g[0].partition_broadcast(P)),
                             (br[:], g.b_router[0].partition_broadcast(P))):
                sp.dma_start(dst, src).then_inc(w_in, 16)

            def body(t, mixes, projects, routes):
                if mixes:
                    held(sp, n_step, (t + 1) * NS, g.passed)
                    held(sp, a_step, (t + 1) * AS, g.passed)
                    sp.dma_start(o_in[:], g.attn[ds((t + 1) * P, P), :]).then_inc(o_arr, 16)
                    held(sp, c_turned, t + 1, g.passed)
                    sp.dma_start(c_in[:], g.convT.rearrange("i p t -> p i t")[:, :, ds((t + 1) * P, P)]
                                 ).then_inc(c_arr, 16)
                if projects:
                    wait(sp, l_step, (t - 1) * LS + 2)
                    if isinstance(t, int) and t == TT - 1:
                        sp.dma_start(x_in[:], g.x_tail).then_inc(x_arr, 16)
                    else:
                        sp.dma_start(x_in[:], g.x_prompt[ds(t * P, P), :]).then_inc(x_arr, 16)
                if routes:
                    sp.wait_ge(l_step, t * LS)
                    sp.dma_start(g.x1[ds((t - 1) * P, P), :], x1[:]).then_inc(x1_out, 16)
            tile_pipeline(sp, body)
            sp.wait_ge(x1_out, 16 * TT)

        @block.tensor
        def _(pe):
            pe.wait_ge(w_in, 16 * 8)

            def body(t, mixes, projects, routes):
                if mixes:
                    pe.wait_ge(c_arr, (t + 1) * 16 + 16)
                    wait(pe, n_step, (t + 1) * NS)
                    for i in range(H):
                        mm = nc.tensor.transpose(c_ps[:, i * P:(i + 1) * P], c_in[:, i, :], g.ident[:])
                    mm.then_inc(c_turned, 1)
                if projects:
                    pe.wait_ge(n_step, (t + 1) * NS)
                    pe.wait_ge(a_step, (t + 1) * AS)
                    for half in range(2):
                        for k in range(4):
                            kk = 4 * half + k
                            mm = nc.tensor.transpose(m_ps[half][:, k * P:(k + 1) * P], mix[:, kk * P:(kk + 1) * P],
                                                     g.ident[:])
                        mm.then_inc(m_turned, 1)
                    pe.wait_ge(m_copied, t * 2 + 2)
                    wait(pe, l_step, (t - 1) * LS + 2)
                    for half in range(2):
                        for k in range(KT):
                            mm = nc.tensor.matmul(p_ps[half][:], mT[:, k, :], wo[:, k, half * 512:(half + 1) * 512],
                                                  start=(k == 0), stop=(k == KT - 1))
                        mm.then_inc(projected, 1)
                if routes:
                    pe.wait_ge(l_step, t * LS)
                    wait(pe, x_copied, (t - 1) * 2)
                    for half in range(2):
                        for k in range(4):
                            kk = 4 * half + k
                            mm = nc.tensor.transpose(x_ps[half][:, k * P:(k + 1) * P], x1[:, kk * P:(kk + 1) * P],
                                                     g.ident[:])
                        mm.then_inc(x_turned, 1)
                    pe.wait_ge(x_copied, t * 2)
                    wait(pe, r_sig, t - 1)
                    for k in range(KT):
                        mm = nc.tensor.matmul(r_ps[:, 0:E], x1T[:, k, :], wr[:, k, :], start=(k == 0),
                                              stop=(k == KT - 1))
                    mm.then_inc(routed, 1)
            tile_pipeline(pe, body)

        @block.scalar
        def _(act):
            act.wait_ge(eps_ready, 1)

            def body(t, mixes, projects, routes):
                if projects:
                    for half in range(2):
                        act.wait_ge(m_turned, t * 2 + (half + 1))
                        nc.scalar.copy(mT[:, 4 * half:4 * half + 4, :],
                                       m_ps[half][:].rearrange("p (k t) -> p k t", k=4)).then_inc(m_copied, 1)
                if routes:
                    act.wait_ge(l_step, (t - 1) * LS + 4)
                    nc.scalar.activation(lrs[:, 0:1], lmv[:, 1:2], ACT.Sqrt, bias=eps[:]).then_inc(l_root, 1)
                if mixes:
                    act.wait_ge(o_arr, (t + 1) * 16 + 16)
                    wait(act, n_step, (t + 1) * NS)
                    for h in range(H):
                        ins = nc.scalar.activation(square[:, h * P:(h + 1) * P], o_in[:, h * P:(h + 1) * P], ACT.Square,
                                                   accum_out=rms[:, h:h + 1])
                        if h == H - 1:
                            ins.then_inc(a_step, 1)
                    act.wait_ge(a_step, (t + 1) * AS + 1)
                    nc.scalar.activation(rms[:], rms[:], ACT.Sqrt, bias=eps[:], scale=1.0 / P).then_inc(a_step, 1)
                    act.wait_ge(n_step, (t + 1) * NS + 2)
                    nc.scalar.activation(crs[:, 0:1], cmv[:, 1:2], ACT.Sqrt, bias=eps[:]).then_inc(a_step, 1)
                    act.wait_ge(n_step, (t + 1) * NS + 6)
                    wait(act, m_turned, (t + 1) * 2)
                    nc.scalar.activation(mix[:, C:D], cn[:], ACT.Silu).then_inc(a_step, 2)
                if routes:
                    for half in range(2):
                        act.wait_ge(x_turned, (t - 1) * 2 + (half + 1))
                        wait(act, routed, t - 1)
                        nc.scalar.copy(x1T[:, 4 * half:4 * half + 4, :],
                                       x_ps[half][:].rearrange("p (k t) -> p k t", k=4)).then_inc(x_copied, 1)
                    act.wait_ge(routed, t)
                    wait(act, r_step, (t - 1) * RS)
                    nc.scalar.activation(sig[:], r_ps[:, 0:E], ACT.Sigmoid).then_inc(r_sig, 1)
            tile_pipeline(act, body)

        @block.vector
        def _(dve):
            nc.vector.memset(eps[:], EPS).then_inc(eps_ready, 1)
            dve.wait_ge(w_in, 16 * 8)
            nc.vector.tensor_scalar(sub[:], sub[:], 1.0 - LAMBDA_INIT, None, ALU.mult).then_inc(eps_ready, 1)
            dve.wait_ge(eps_ready, 2)

            def norms(t):
                b = t * NS
                dve.wait_ge(c_turned, t + 1)
                nc.vector.bn_stats(cst[:], c_ps[:]).then_inc(n_step, 1)
                held(dve, n_step, b + 1, g.passed)
                nc.vector.bn_aggr(cmv[:], cst[:]).then_inc(n_step, 1)
                dve.wait_ge(a_step, t * AS + 3)
                nc.vector.reciprocal(crs[:, 1:2], crs[:, 0:1]).then_inc(n_step, 1)
                dve.wait_ge(n_step, b + 3)
                nc.vector.tensor_scalar(cn[:], c_ps[:], cmv[:, 0:1], crs[:, 1:2], ALU.subtract, ALU.mult
                                        ).then_inc(n_step, 1)
                dve.wait_ge(n_step, b + 4)
                nc.vector.tensor_tensor(cn[:], cn[:], cg[:], ALU.mult).then_inc(n_step, 1)
                dve.wait_ge(n_step, b + 5)
                nc.vector.tensor_tensor(cn[:], cn[:], cb[:], ALU.add).then_inc(n_step, 1)
                nc.vector.reciprocal(rstd[:], rms[:]).then_inc(n_step, 1)
                dve.wait_ge(n_step, b + 7)
                wait(dve, m_turned, t * 2)
                for h in range(H):
                    ins = nc.vector.scalar_tensor_tensor(out=mix[:, h * P:(h + 1) * P], in0=o_in[:, h * P:(h + 1) * P],
                                                         scalar=rstd[:, h:h + 1], in1=sub[:], op0=ALU.mult,
                                                         op1=ALU.mult)
                ins.then_inc(n_step, 3)

            def layer_norm(t):
                b = t * LS
                dve.wait_ge(x_arr, t * 16 + 16)
                for half in range(2):
                    dve.wait_ge(projected, t * 2 + (half + 1))
                    at = slice(half * 512, (half + 1) * 512)
                    nc.vector.scalar_tensor_tensor(out=res[:, at], in0=x_in[:, at], scalar=ALPHA, in1=p_ps[half][:],
                                                   op0=ALU.mult, op1=ALU.add).then_inc(l_step, 1)
                for half in range(2):
                    dve.wait_ge(l_step, b + (half + 1))
                    ins = nc.vector.bn_stats(lst[:, half, :], res[:, half * 512:(half + 1) * 512])
                ins.then_inc(l_step, 1)
                held(dve, l_step, b + 3, g.passed)
                nc.vector.bn_aggr(lmv[:], lst[:].rearrange("p a b -> p (a b)")).then_inc(l_step, 1)
                dve.wait_ge(l_root, t + 1)
                nc.vector.reciprocal(lrs[:, 1:2], lrs[:, 0:1]).then_inc(l_step, 1)
                dve.wait_ge(l_step, b + 5)
                nc.vector.tensor_scalar(res[:], res[:], lmv[:, 0:1], lrs[:, 1:2], ALU.subtract, ALU.mult
                                        ).then_inc(l_step, 1)
                dve.wait_ge(l_step, b + 6)
                nc.vector.tensor_tensor(res[:], res[:], ln_g[:], ALU.mult).then_inc(l_step, 1)
                dve.wait_ge(l_step, b + 7)
                wait(dve, x_turned, t * 2)
                wait(dve, x1_out, t * 16)
                nc.vector.tensor_tensor(x1[:], res[:], ln_b[:], ALU.add).then_inc(l_step, 1)

            def route(t):
                n = [0]

                def step(ins):
                    ins.then_inc(r_step, 1)
                    n[0] += 1

                def settled():
                    held(dve, r_step, t * RS + n[0], g.passed)
                dve.wait_ge(r_sig, t + 1)
                step(nc.vector.tensor_tensor(sel[:], sig[:], br[:], ALU.add))
                settled()
                for k in range(EG):
                    step(nc.vector.max(out=srt[:, k, :], in_=sel[:, k * EG:(k + 1) * EG]))
                settled()
                step(nc.vector.tensor_tensor(gs[:], srt[:, :, 0], srt[:, :, 1], ALU.add))
                settled()
                step(nc.vector.max(out=g8[:], in_=gs[:]))
                settled()
                step(nc.vector.max_index(out=gi[:], in_max=g8[:], in_values=gs[:]))
                settled()
                step(nc.vector.tensor_copy(gf[:], gi[:]))
                settled()
                step(nc.vector.tensor_tensor(eq[:], g.iota_e[:, 0:EG].unsqueeze(2).to_broadcast([P, EG, TOPG]),
                                             gf[:, 0:TOPG].unsqueeze(1).to_broadcast([P, EG, TOPG]), ALU.is_equal))
                settled()
                step(nc.vector.tensor_reduce(gm[:], eq[:], AX.X, ALU.add))
                settled()
                step(nc.vector.tensor_scalar(pen[:], gm[:], -1.0, -NEG, ALU.add, ALU.mult))
                step(nc.vector.tensor_tensor(sel[:].rearrange("p (g e) -> p g e", g=EG),
                                             sel[:].rearrange("p (g e) -> p g e", g=EG),
                                             gm[:].unsqueeze(2).to_broadcast([P, EG, E // EG]), ALU.mult))
                settled()
                step(nc.vector.tensor_tensor(sel[:].rearrange("p (g e) -> p g e", g=EG),
                                             sel[:].rearrange("p (g e) -> p g e", g=EG),
                                             pen[:].unsqueeze(2).to_broadcast([P, EG, E // EG]), ALU.add))
                settled()
                step(nc.vector.max(out=v8[:], in_=sel[:]))
                settled()
                step(nc.vector.match_replace(out=picked[:], in_to_replace=v8[:], in_values=sel[:], imm_value=-NEG))
                settled()
                step(nc.vector.tensor_scalar(hit[:], picked[:], -NEG, None, ALU.is_equal))
                settled()
                step(nc.vector.scalar_tensor_tensor(out=w[:], in0=sig[:], scalar=1.0, in1=hit[:], op0=ALU.mult,
                                                    op1=ALU.mult, accum_out=ws[:]))
                step(nc.vector.tensor_scalar(g.chosen[:, ds(t, 1), :].rearrange("p a e -> p (a e)"), hit[:],
                                             g.valid[:, ds(t, 1)], None, ALU.mult))
                settled()
                step(nc.vector.reciprocal(wrec[:], ws[:]))
                settled()
                step(nc.vector.tensor_scalar(g.weight[:, ds(t, 1), :].rearrange("p a e -> p (a e)"), w[:], wrec[:],
                                             ROUTED_SCALE, ALU.mult, ALU.mult))
                assert n[0] == RS, n[0]

            def body(t, mixes, projects, routes):
                if mixes:
                    norms(t + 1)
                if projects:
                    layer_norm(t)
                if routes:
                    route(t - 1)
            tile_pipeline(dve, body)


SH = TT
SLOTS = TOK * TOPK
NBLK = SH + (SLOTS + E * P) // P + 1


def plan_dispatch(nc, g):
    with ExitStack() as ctx:
        sb = lambda n, s, dt=F32: ctx.enter_context(nc.sbuf_tensor(n, s, dt))
        bf = sb("chosen_bf", [P, TT, E], BF16)
        tri, ones = sb("earlier", [P, P], BF16), sb("ones_bf", [P, P], BF16)
        before = sb("before_tile", [P, TT + 1, E])
        count_i, blocks, one = sb("count_int", [P, E], I32), sb("blocks", [P, E]), sb("ones_row", [P, E])
        upto, base = sb("blocks_upto", [P, E]), sb("base_row", [P, E])
        rowno = sb("row_plus1", [P, TT, E])
        d8 = sb("row8_f", [P, TT, TOPK])
        match = sb("match", [P, TT, TOPK, E])
        lo, hi = sb("row_low", [P, TT * TOPK], I32), sb("row_high", [P, TT * TOPK], I32)
        zero_table = sb("zero_table", [P, NBLK], U32)
        chunks = [(0, 8), (8, 8), (16, 1)]
        r_ps = [ctx.enter_context(nc.psum_tensor(f"rank_ps{c}", [P, 512], F32)) for c in range(3)]
        c_ps = [ctx.enter_context(nc.psum_tensor(f"count_ps{c}", [P, 512], F32)) for c in range(3)]
        const_ready, bf_ready, ranked, step, table_out = sems(nc, ctx, "pd_const", "pd_bf", "pd_ranked", "pd_step",
                                                             "table_out")
        block = ctx.enter_context(nc.Block())

        @block.gpsimd
        def _(pool):
            nc.gpsimd.memset(zero_table[:], 0).then_inc(const_ready, 1)
            nc.gpsimd.memset(ones[:], 1.0).then_inc(const_ready, 1)
            nc.gpsimd.memset(tri[:], 1.0).then_inc(const_ready, 1)
            pool.wait_ge(const_ready, 3)
            nc.gpsimd.affine_select(out=tri[:], in_=tri[:], compare_op=ALU.is_gt, fill=0.0, base=0,
                                    pattern=[[1, P]], channel_multiplier=-1).then_inc(const_ready, 1)
            pool.dma_start(g.slot_token.rearrange("(p b) -> p b", p=P), zero_table[:]).then_inc(table_out, 16)
            pool.wait_ge(table_out, 16)

        @block.tensor
        def _(pe):
            pe.wait_ge(const_ready, 4)
            pe.wait_ge(bf_ready, 1)
            for ps, lhs in ((c_ps, ones), (r_ps, tri)):
                for c, (t, n) in enumerate(chunks):
                    nc.tensor.matmul(ps[c][:, 0:n * E], lhs[:], bf[:, t:t + n, :].rearrange("p t e -> p (t e)"),
                                     start=True, stop=True).then_inc(ranked, 1)

        @block.vector
        def _(dve):
            n = [0]

            def then(ins):
                ins.then_inc(step, 1)
                n[0] += 1
                dve.wait_ge(step, n[0])
            nc.vector.tensor_copy(bf[:], g.chosen[:]).then_inc(bf_ready, 1)
            then(nc.vector.memset(one[:], 1.0))
            then(nc.vector.memset(before[:, 0, :], 0.0))
            dve.wait_ge(ranked, 3)
            for t in range(TT):
                then(nc.vector.tensor_tensor(before[:, t + 1, :], before[:, t, :],
                                             c_ps[t // 8][:, (t % 8) * E:(t % 8 + 1) * E], ALU.add))
            then(nc.vector.tensor_scalar(count_i[:], before[:, TT, :], float(P - 1), None, ALU.add))
            then(nc.vector.tensor_scalar(count_i[:], count_i[:], 7, None, ALU.logical_shift_right))
            then(nc.vector.tensor_scalar(blocks[:], count_i[:], 1.0, None, ALU.max))
            then(nc.vector.tensor_tensor_scan(upto[:], one[:], blocks[:], float(SH), ALU.mult, ALU.add))
            then(nc.vector.memset(g.bounds[:, 0:1], SH))
            then(nc.vector.tensor_copy(g.bounds[:, 1:E + 1], upto[0:1, :]))
            then(nc.vector.tensor_scalar(g.bounds[:, E + 1:E + 2], upto[0:1, E - 1:E], -1.0, float(NBLK), ALU.mult,
                                         ALU.add))
            then(nc.vector.tensor_tensor(base[:], upto[:], blocks[:], ALU.subtract))
            then(nc.vector.tensor_scalar(base[:], base[:], float(P), 1.0, ALU.mult, ALU.add))
            dve.wait_ge(ranked, 6)
            for c, (t, m) in enumerate(chunks):
                then(nc.vector.tensor_tensor(rowno[:, t:t + m, :], before[:, t:t + m, :],
                                             r_ps[c][:, 0:m * E].rearrange("p (t e) -> p t e", e=E), ALU.add))
            then(nc.vector.tensor_tensor(rowno[:], rowno[:], base[:].unsqueeze(1).to_broadcast([P, TT, E]), ALU.add))
            then(nc.vector.tensor_tensor(rowno[:], rowno[:], g.chosen[:], ALU.mult))
            for t in range(TT):
                ins = nc.vector.max(out=d8[:, t, :], in_=rowno[:, t, :])
            then(ins)
            b4 = [P, TT, TOPK, E]
            then(nc.vector.tensor_tensor(match[:], rowno[:].unsqueeze(2).to_broadcast(b4),
                                         d8[:].unsqueeze(3).to_broadcast(b4), ALU.is_equal))
            then(nc.vector.tensor_tensor(match[:], match[:], g.weight[:].unsqueeze(2).to_broadcast(b4), ALU.mult))
            then(nc.vector.tensor_reduce(g.weight8[:], match[:], AX.X, ALU.add))
            then(nc.vector.tensor_scalar(g.row8[:], d8[:], -1.0, None, ALU.add))
            r = g.row8[:].rearrange("p t k -> p (t k)")
            then(nc.vector.tensor_scalar(lo[:], r, P - 1, None, ALU.bitwise_and))
            then(nc.vector.tensor_scalar(hi[:], r, 7, None, ALU.arith_shift_right))
            then(nc.vector.scalar_tensor_tensor(out=g.place8[:].rearrange("p t k -> p (t k)"), in0=lo[:],
                                                scalar=float(NBLK), in1=hi[:], op0=ALU.mult, op1=ALU.add))


F = 256


def experts(nc, g):
    with ExitStack() as ctx:
        sb = lambda n, s, dt=F32: ctx.enter_context(nc.sbuf_tensor(n, s, dt))
        token = sb("token_no", [P, TT], U32)
        index = sb("gather_index", [P, NBLK + 1], U32)
        now = sb("gather_now", [P, 1], U32)
        W = 3 * 2 * D
        part_of = lambda which: slice(which * 2 * D, (which + 1) * 2 * D)
        raw = [sb(f"w_raw{u}", [P, W]) for u in range(2)]
        high = [sb(f"w_high{u}", [P, W], F32R) for u in range(2)]
        low = [sb(f"w_low{u}", [P, W], F32R) for u in range(2)]
        xg = sb("x_rows", [P, D])
        x_high, x_low = sb("x_highT", [P, KT, P], F32R), sb("x_lowT", [P, KT, P], F32R)
        h_high, h_low = sb("h_highT", [P, F // P, P], F32R), sb("h_lowT", [P, F // P, P], F32R)
        sg, hid, y = sb("silu_gate", [P, F]), sb("hidden", [P, F]), sb("y_rows", [P, D])
        zero = sb("zero_rows", [P, D])
        bank = lambda n: ctx.enter_context(nc.psum_tensor(n, [P, 512], F32))
        g_ps, u_ps, h_ps = bank("gate_ps"), bank("up_ps"), bank("hid_ps")
        x_ps, y_ps = [bank(f"xr_ps{i}") for i in range(2)], [bank(f"y_ps{i}") for i in range(2)]
        (token_ready, scattered, index_ready, now_ready, x_arr, x_turned, xt_high, xt_low, raw_in0, raw_in1, w_high, w_low, wd_low,
         picked_ready, gated, upped, silu_ready, h_ready, h_turned, h_high_kept, h_low_kept, downed, y_act, y_dve,
         y_out, zero_ready, filled) = sems(
            nc, ctx, "token_ready", "scattered", "index_ready", "now_ready", "xr_arrived", "xr_turned", "xt_high",
            "xt_low", "w_raw_in0", "w_raw_in1", "w_high_ready", "w_low_ready", "wd_low_ready", "picked_ready", "gated", "upped", "silu_ready",
            "h_ready", "h_turned", "h_high_kept", "h_low_kept", "downed", "y_act", "y_dve", "y_out", "zero_ready",
            "filled")
        raw_in = (raw_in0, raw_in1)
        W_DMAS = 3 * 16
        PIECE = [slice(n * D, (n + 1) * D) for n in range(4)]
        HIGHS, LOWS = len(PIECE) + 1, len(PIECE)

        def blocks(eng, block, begin=lambda j, ahead, u, lower, i=0: None):
            block(0, 0)
            with eng.Fori(1, SH - 2) as n:
                block(n, 0)
            block(SH - 2, 0)
            begin(0, E, 0, None)
            block(SH - 1, 0)

            def pair(i, ahead):
                for u in (1, 0):
                    _, (lower, upper) = nc.values_load_multi_w_load_instructions(
                        g.bounds[0:1, ds(i * 2 + (1 - u), 2)], (eng.engine,), min_val=SH, max_val=NBLK - 1)
                    begin(i * 2 + (2 - u), ahead - 1 + u, u, lower, i)
                    with eng.Fori(lower, upper) as n:
                        block(n, u)
            with eng.Fori(0, E // 2 - 1) as i:
                pair(i, 3)
            pair(E // 2 - 1, 1)

        block = ctx.enter_context(nc.Block())

        @block.sync
        def _(sp):
            def load(u, gate, up, down):
                for which, w in enumerate((gate, up, down)):
                    sp.dma_start(raw[u][:, part_of(which)].rearrange("p (k f) -> p k f", f=w.shape[-1]),
                                 w.rearrange("(k p) f -> p k f", p=P)).then_inc(raw_in[u], 16)

            load(0, g.w_sh_gate[0], g.w_sh_up[0], g.w_sh_down[0])
            load(1, g.w_gate[0, 0], g.w_up[0, 0], g.w_down[0, 0])
            _, (last,) = nc.values_load_multi_w_load_instructions(g.bounds[0:1, E:E + 1], (sp.engine,), min_val=SH,
                                                                  max_val=NBLK - 1)
            sp.wait_ge(zero_ready, 1)
            with sp.Fori(last, NBLK) as n:
                sp.dma_start(g.y[ds(n * P, P), :], zero[:]).then_inc(filled, 16)

            def begin(j, ahead, u, lower, i=0):
                if ahead < 2:
                    return
                held(sp, w_low, j * LOWS + LOWS, g.passed)
                held(sp, wd_low, j + 1, g.passed)
                if isinstance(j, int):
                    load(u, g.w_gate[0, j + 1], g.w_up[0, j + 1], g.w_down[0, j + 1])
                else:
                    load(u, *(t[0][ds(j + 1, 1)].rearrange("a r c -> (a r) c") for t in (g.w_gate, g.w_up, g.w_down)))

            def store(n, u):
                sp.wait_ge(y_act, n + 1)
                sp.wait_ge(y_dve, n + 1)
                sp.dma_start(g.y[ds(n * P, P), :], y[:]).then_inc(y_out, 16)
            blocks(sp, store, begin)
            held(sp, y_out, last * 16, g.passed)
            _, (unused,) = nc.values_load_multi_w_load_instructions(g.bounds[0:1, E + 1:E + 2], (sp.engine,),
                                                                    min_val=1, max_val=NBLK)
            held(sp, filled, unused * 16, g.passed)

        @block.gpsimd
        def _(pool):
            nc.gpsimd.iota(token[:], pattern=[[P, TT]], base=0, channel_multiplier=1).then_inc(token_ready, 1)
            nc.gpsimd.memset(index[:, NBLK:NBLK + 1], 0).then_inc(token_ready, 1)
            pool.wait_ge(token_ready, 2)

            def gather(n):
                held(pool, now_ready, n + 1, g.passed)
                pool.indirect_dma_start(out=xg[:], out_offset=None, in_=g.x1,
                                        in_offset=bass.IndirectOffsetOnAxis(ap=now[:], axis=0)).then_inc(x_arr, 16)

            def split_down(j, u):
                pool.wait_ge(w_high, j * HIGHS + HIGHS)
                nc.gpsimd.tensor_tensor(low[u][:, part_of(2)], raw[u][:, part_of(2)], high[u][:, part_of(2)],
                                        ALU.subtract).then_inc(wd_low, 1)

            for n in range(SH):
                gather(n)
                if n == 0:
                    split_down(0, 0)
                rows = P if n < QT else TAIL
                for k in range(TOPK):
                    pool.indirect_dma_start(
                        out=g.slot_token.rearrange("(s a) -> s a", a=1),
                        out_offset=bass.IndirectOffsetOnAxis(ap=g.place8[0:rows, n, k:k + 1], axis=0),
                        in_=token[0:rows, n:n + 1], in_offset=None).then_inc(scattered, 16)
            pool.wait_ge(scattered, 16 * SH * TOPK)
            pool.dma_start(index[:, SH:NBLK], g.slot_token.rearrange("(p b) -> p b", p=P)[:, SH:NBLK]
                           ).then_inc(index_ready, 16)
            gather(SH)
            split_down(1, 1)
            gather(SH + 1)

            def pair(i, ahead):
                for u in (1, 0):
                    _, (lower, upper) = nc.values_load_multi_w_load_instructions(
                        g.bounds[0:1, ds(i * 2 + (1 - u), 2)], (pool.engine,), min_val=SH, max_val=NBLK - 1)
                    if ahead - 1 + u:
                        split_down(i * 2 + (3 - u), 1 - u)
                    with pool.Fori(lower, upper) as n:
                        gather(n + 2)
            with pool.Fori(0, E // 2 - 1) as i:
                pair(i, 3)
            pair(E // 2 - 1, 1)
            _, (last,) = nc.values_load_multi_w_load_instructions(g.bounds[0:1, E:E + 1], (pool.engine,), min_val=SH,
                                                                  max_val=NBLK - 1)
            held(pool, x_arr, last * 16 + 32, g.passed)

        @block.tensor
        def _(pe):
            def turn(n, half):
                if half == 0:
                    pe.wait_ge(x_arr, n * 16 + 16)
                for k in range(4):
                    kk = 4 * half + k
                    mm = nc.tensor.transpose(x_ps[half][:, k * P:(k + 1) * P], xg[:, kk * P:(kk + 1) * P],
                                             g.ident[:])
                mm.then_inc(x_turned, 1)
            turn(0, 0)
            turn(0, 1)

            def products(n, u):
                pe.wait_ge(xt_low, n * 2 + 2)
                for ps, which, done in ((g_ps, 0, gated), (u_ps, 1, upped)):
                    for k in range(KT):
                        at = slice(which * 2 * D + k * F, which * 2 * D + (k + 1) * F)
                        nc.tensor.matmul(ps[:, 0:F], x_high[:, k, :], high[u][:, at], start=(k == 0), stop=False)
                        nc.tensor.matmul(ps[:, 0:F], x_high[:, k, :], low[u][:, at], start=False, stop=False)
                        mm = nc.tensor.matmul(ps[:, 0:F], x_low[:, k, :], high[u][:, at], start=False,
                                              stop=(k == KT - 1))
                    mm.then_inc(done, 1)
                turn(n + 1, 0)
                pe.wait_ge(h_ready, n + 1)
                for k in range(F // P):
                    mm = nc.tensor.transpose(h_ps[:, k * P:(k + 1) * P], hid[:, k * P:(k + 1) * P], g.ident[:])
                mm.then_inc(h_turned, 1)
                turn(n + 1, 1)
                pe.wait_ge(h_high_kept, n + 1)
                wait(pe, y_act, n)
                wait(pe, y_dve, n)
                down = lambda half, k: slice(4 * D + k * D + half * 512, 4 * D + k * D + (half + 1) * 512)
                for half in range(2):
                    for k in range(F // P):
                        for w in (high, low):
                            nc.tensor.matmul(y_ps[half][:], h_high[:, k, :], w[u][:, down(half, k)],
                                             start=(k == 0 and w is high), stop=False)
                pe.wait_ge(h_low_kept, n + 1)
                for half in range(2):
                    for k in range(F // P):
                        mm = nc.tensor.matmul(y_ps[half][:], h_low[:, k, :], high[u][:, down(half, k)],
                                              start=False, stop=(k == F // P - 1))
                    mm.then_inc(downed, 1)

            def begin(j, ahead, u, lower, i=0):
                if lower is not None:
                    held(pe, w_low, j * LOWS + LOWS, g.passed)
                    held(pe, wd_low, j + 1, g.passed)
            pe.wait_ge(w_low, LOWS)
            pe.wait_ge(wd_low, 1)
            blocks(pe, products, begin)

        @block.scalar
        def _(act):
            def turned(n, half):
                act.wait_ge(x_turned, n * 2 + (half + 1))
                nc.scalar.copy(x_high[:, 4 * half:4 * half + 4, :], x_ps[half][:].rearrange("p (k t) -> p k t", k=4)
                               ).then_inc(xt_high, 1)

            def split(j, loads, u):
                act.wait_ge(raw_in[u], loads * W_DMAS)
                for at in (*PIECE, part_of(2)):
                    nc.scalar.copy(high[u][:, at], raw[u][:, at]).then_inc(w_high, 1)
            split(0, 1, 0)
            turned(0, 0)
            turned(0, 1)

            def begin(j, ahead, u, lower, i=0):
                if ahead:
                    if lower is not None:
                        act.wait_ge(downed, lower * 2)
                    split(j + 1, i + (1 if lower is None else 2), 1 - u)

            def body(n, u):
                act.wait_ge(gated, n + 1)
                wait(act, h_ready, n)
                nc.scalar.activation(sg[:], g_ps[:, 0:F], ACT.Silu).then_inc(silu_ready, 1)
                turned(n + 1, 0)
                act.wait_ge(h_turned, n + 1)
                nc.scalar.copy(h_high[:], h_ps[:, 0:F].rearrange("p (k t) -> p k t", k=F // P)
                               ).then_inc(h_high_kept, 1)
                turned(n + 1, 1)
                act.wait_ge(downed, n * 2 + 1)
                wait(act, y_out, n * 16)
                nc.scalar.copy(y[:, 0:512], y_ps[0][:]).then_inc(y_act, 1)
            blocks(act, body, begin)

        @block.vector
        def _(dve):
            def pick(n):
                nc.vector.tensor_copy(now[:], index[:, ds(n, 1)]).then_inc(now_ready, 1)

            def turned(n, half):
                dve.wait_ge(xt_high, n * 2 + (half + 1))
                at = slice(4 * half, 4 * half + 4)
                nc.vector.tensor_tensor(x_low[:, at, :], x_ps[half][:].rearrange("p (k t) -> p k t", k=4),
                                        x_high[:, at, :], ALU.subtract).then_inc(xt_low, 1)

            def split(j, u):
                for n, at in enumerate(PIECE):
                    dve.wait_ge(w_high, j * HIGHS + (n + 1))
                    nc.vector.tensor_tensor(low[u][:, at], raw[u][:, at], high[u][:, at], ALU.subtract
                                            ).then_inc(w_low, 1)

            def begin(j, ahead, u, lower, i=0):
                if ahead:
                    split(j + 1, 1 - u)
            split(0, 0)
            dve.wait_ge(token_ready, 2)
            nc.vector.memset(zero[:], 0.0).then_inc(zero_ready, 1)
            nc.vector.tensor_copy(index[:, 0:SH], token[:]).then_inc(picked_ready, 1)
            dve.wait_ge(picked_ready, 1)
            pick(0)
            turned(0, 0)
            turned(0, 1)
            pick(1)

            def body(n, u):
                dve.wait_ge(silu_ready, n + 1)
                dve.wait_ge(upped, n + 1)
                nc.vector.tensor_tensor(hid[:], sg[:], u_ps[:, 0:F], ALU.mult).then_inc(h_ready, 1)
                turned(n + 1, 0)
                dve.wait_ge(h_high_kept, n + 1)
                nc.vector.tensor_tensor(h_low[:], h_ps[:, 0:F].rearrange("p (k t) -> p k t", k=F // P), h_high[:],
                                        ALU.subtract).then_inc(h_low_kept, 1)
                turned(n + 1, 1)
                if isinstance(n, int) and n == SH - 2:
                    dve.wait_ge(index_ready, 16)
                pick(n + 2)
                dve.wait_ge(downed, n * 2 + 2)
                wait(dve, y_out, n * 16)
                nc.vector.tensor_copy(y[:, 512:D], y_ps[1][:]).then_inc(y_dve, 1)
            blocks(dve, body, begin)


def combine(nc, g):
    with ExitStack() as ctx:
        sb = lambda n, s, dt=F32: ctx.enter_context(nc.sbuf_tensor(n, s, dt))
        ln_g, ln_b = sb("ln2_g", [P, D]), sb("ln2_b", [P, D])
        row = [[sb(f"y_row{u}_{k}", [P, D]) for k in range(TOPK)] for u in range(2)]
        res, acc = [sb(f"x1_row{u}", [P, D]) for u in range(2)], [sb(f"y_shared{u}", [P, D]) for u in range(2)]
        out = [sb(f"y_tile{u}", [P, D]) for u in range(2)]
        st, mv, rs, eps = sb("l2_stats", [P, 2, 6]), sb("l2_meanvar", [P, 2]), sb("l2_rstd", [P, 2]), sb("eps2", [P, 1])
        w_in, eps_ready, rows0, rows1, tile0, tile1, step, root, out0, out1 = sems(
            nc, ctx, "p6_w_in", "eps2_ready", "rows_in0", "rows_in1", "tile_in0", "tile_in1", "comb_step", "comb_root",
            "y_out0", "y_out1")
        rows_in, tile_in, stored = (rows0, rows1), (tile0, tile1), (out0, out1)
        STEPS = TOPK + 7
        block = ctx.enter_context(nc.Block())

        def tiles(eng, body):
            def pair(i):
                for u in range(2):
                    body(i, u, P)
            loop(eng, QT // 2, pair)
            body(QT // 2, 0, TAIL)

        @block.sync
        def _(sp):
            sp.dma_start(ln_g[:], g.ln2_g[0].partition_broadcast(P)).then_inc(w_in, 16)
            sp.dma_start(ln_b[:], g.ln2_b[0].partition_broadcast(P)).then_inc(w_in, 16)

            def read(i, u, n):
                wait(sp, step, (2 * i + (u - 2)) * STEPS + TOPK + 1)
                at = ds(i * (2 * P) + u * P, n)
                sp.dma_start(res[u][0:n, :], g.x1[at, :]).then_inc(tile_in[u], 16)
                wait(sp, step, (2 * i + (u - 1)) * STEPS)
                sp.dma_start(acc[u][0:n, :], g.y[at, :]).then_inc(tile_in[u], 16)

            def write(i, u, n):
                sp.wait_ge(step, (2 * i + (u + 1)) * STEPS)
                to = g.y_sample if n == TAIL else g.y_prompt[ds(i * (2 * P) + u * P, P), :]
                sp.dma_start(to, out[u][0:n, :]).then_inc(stored[u], 16)
            read(0, 0, P)

            def body(i):
                for u in range(2):
                    if u == 0:
                        read(i, 1, P)
                    else:
                        read(i + 1, 0, P)
                    write(i, u, P)
            loop(sp, QT // 2 - 1, body)
            read(QT // 2 - 1, 1, P)
            write(QT // 2 - 1, 0, P)
            read(QT // 2, 0, TAIL)
            write(QT // 2 - 1, 1, P)
            write(QT // 2, 0, TAIL)
            sp.wait_ge(stored[0], 16 * (QT // 2 + 1))
            sp.wait_ge(stored[1], 16 * (QT // 2))

        @block.gpsimd
        def _(pool):
            for t in range(TT):
                u, n = t % 2, P if t < QT else TAIL
                for k in range(TOPK):
                    wait(pool, step, (t - 2) * STEPS + k + 1)
                    pool.indirect_dma_start(out=row[u][k][0:n, :], out_offset=None, in_=g.y,
                                            in_offset=bass.IndirectOffsetOnAxis(
                                                ap=g.row8[:].bitcast(U32)[0:n, t, k:k + 1], axis=0)
                                            ).then_inc(rows_in[u], 16)

        @block.scalar
        def _(act):
            act.wait_ge(eps_ready, 1)

            def body(i, u, n):
                act.wait_ge(step, (2 * i + u) * STEPS + TOPK + 3)
                nc.scalar.activation(rs[0:n, 0:1], mv[0:n, 1:2], ACT.Sqrt, bias=eps[0:n, :]).then_inc(root, 1)
            tiles(act, body)

        @block.vector
        def _(dve):
            nc.vector.memset(eps[:], EPS).then_inc(eps_ready, 1)
            dve.wait_ge(w_in, 32)

            def body(i, u, n):
                b = (2 * i + u) * STEPS
                a = acc[u][0:n, :]
                dve.wait_ge(tile_in[u], i * 32 + 32)
                dve.wait_ge(rows_in[u], i * (16 * TOPK) + 16 * TOPK)
                for k in range(TOPK):
                    nc.vector.scalar_tensor_tensor(
                        out=a, in0=row[u][k][0:n, :], scalar=g.weight8[0:n, ds(i * 2 + u, 1), k:k + 1].rearrange(
                            "p a b -> p (a b)"), in1=a, op0=ALU.mult, op1=ALU.add).then_inc(step, 1)
                    dve.wait_ge(step, b + (k + 1))
                nc.vector.scalar_tensor_tensor(out=a, in0=res[u][0:n, :], scalar=ALPHA, in1=a, op0=ALU.mult,
                                               op1=ALU.add).then_inc(step, 1)
                dve.wait_ge(step, b + (TOPK + 1))
                for half in range(2):
                    ins = nc.vector.bn_stats(st[0:n, half, :], acc[u][0:n, half * 512:(half + 1) * 512])
                ins.then_inc(step, 1)
                held(dve, step, b + (TOPK + 2), g.passed)
                nc.vector.bn_aggr(mv[0:n, :], st[0:n].rearrange("p a b -> p (a b)")).then_inc(step, 1)
                dve.wait_ge(root, i * 2 + (u + 1))
                nc.vector.reciprocal(rs[0:n, 1:2], rs[0:n, 0:1]).then_inc(step, 1)
                dve.wait_ge(step, b + (TOPK + 4))
                nc.vector.tensor_scalar(a, a, mv[0:n, 0:1], rs[0:n, 1:2], ALU.subtract, ALU.mult).then_inc(step, 1)
                dve.wait_ge(step, b + (TOPK + 5))
                nc.vector.tensor_tensor(a, a, ln_g[0:n, :], ALU.mult).then_inc(step, 1)
                dve.wait_ge(step, b + (TOPK + 6))
                wait(dve, stored[u], i * 16)
                nc.vector.tensor_tensor(out[u][0:n, :], a, ln_b[0:n, :], ALU.add).then_inc(step, 1)
            tiles(dve, body)


PHASES = [constants, mixing_weight, in_projection, prompt_attention, decode_attention, mix_and_route, plan_dispatch, experts, combine]

class Tensors:
    pass


def build(nc, inputs, outputs):
    g = Tensors()
    (g.x_prompt, g.x_sample, g.cache_k, g.cache_v, g.state_conv, g.page_table, g.w_in, g.lam_q1, g.lam_k1, g.lam_q2,
     g.lam_k2, g.subln_g, g.w_dw, g.b_dw, g.conv_ln_g, g.conv_ln_b, g.w_o, g.ln1_g, g.ln1_b, g.w_router, g.b_router,
     g.w_gate, g.w_up, g.w_down, g.w_sh_gate, g.w_sh_up, g.w_sh_down, g.ln2_g, g.ln2_b) = inputs
    (g.y_prompt, g.y_sample, g.k_prompt, g.v_prompt, g.conv_prompt, g.k_sample, g.v_sample, g.conv_sample) = outputs
    g.x_prompt = g.x_prompt.rearrange("b s d -> (b s) d")
    g.x_sample = g.x_sample.rearrange("b s d -> (b s) d")
    g.y_prompt = g.y_prompt.rearrange("b s d -> (b s) d")
    g.y_sample = g.y_sample.rearrange("b s d -> (b s) d")
    g.w_in = g.w_in.rearrange("l d e -> (l d) e")
    g.k_prompt, g.v_prompt, g.k_sample, g.v_sample = (
        t.rearrange("l b s h d -> (l b s) (h d)") for t in (g.k_prompt, g.v_prompt, g.k_sample, g.v_sample))
    scratch = lambda n, s, dt=F32: nc.dram_tensor(n, s, dt, kind="Internal").ap()
    g.x_tail = scratch("x_tail", [P, D])
    g.qT = scratch("qT_s", [H, P, TP])
    g.kT = scratch("kT_s", [H, P, TP])
    g.convT = scratch("convT_s", [H, P, TP])
    g.conv_prompt = g.conv_prompt.rearrange("l b r c -> (l b r) c")
    g.conv_sample = g.conv_sample[0]
    g.attn = scratch("attn_s", [TP, C])
    g.x1 = scratch("x1_s", [TP, D])
    g.y = scratch("y_s", [NBLK * P, D])
    g.slot_token = scratch("slot_token", [P * NBLK], U32)
    with ExitStack() as ctx:
        g.passed, = sems(nc, ctx, "passed")
        sb = lambda n, s, dt=F32: ctx.enter_context(nc.sbuf_tensor(n, s, dt))
        g.ident = sb("ident", [P, P])
        g.ident_bf = sb("ident_bf", [P, P], BF16)
        g.causal = sb("causal", [P, P], BF16)
        g.neg_lam = sb("neg_lam", [P, 1])
        g.valid = sb("valid", [P, TT])
        g.iota_e = sb("iota_e", [P, 8])
        g.chosen = sb("chosen", [P, TT, E])
        g.weight = sb("weight", [P, TT, E])
        g.weight8 = sb("weight8", [P, TT, TOPK])
        g.row8 = sb("row8", [P, TT, TOPK], I32)
        g.place8 = sb("place8", [P, TT, TOPK], U32)
        g.bounds = sb("bounds", [1, E + 2], I32)
        for phase in PHASES:
            phase(nc, g)


_INS = ["x_prompt", "x_sample", "cache_k", "cache_v", "state_conv", "page_table", "w_in", "lam_q1", "lam_k1",
        "lam_q2", "lam_k2", "subln_g", "w_dw", "b_dw", "conv_ln_g", "conv_ln_b", "w_o", "ln1_g", "ln1_b", "w_router",
        "b_router", "w_gate", "w_up", "w_down", "w_sh_gate", "w_sh_up", "w_sh_down", "ln2_g", "ln2_b"]
_OUTS = [(1, SEQ, D), (NSEQ, NEW, D), (1, 1, SEQ, H, P), (1, 1, SEQ, H, P), (1, 1, 30, C),
         (1, NSEQ, NEW, H, P), (1, NSEQ, NEW, H, P), (1, NSEQ, 30, C)]


def kernel(**inputs):
    import numpy as _np
    import concourse.bacc as _bacc
    from concourse import mybir as _mybir
    from concourse.bass_utils import run_bass_kernel_spmd as _run

    nc = _bacc.Bacc("TRN2", target_bir_lowering=False, num_devices=1)
    arrays, ins, outs = {}, [], []
    for name in _INS:
        a = _np.ascontiguousarray(inputs[name])
        arrays[f"in_{name}_dram"] = a
        ins.append(nc.dram_tensor(f"in_{name}_dram", a.shape, _mybir.dt.from_np(a.dtype), kind="ExternalInput").ap())
    for i, shape in enumerate(_OUTS):
        outs.append(nc.dram_tensor(f"out_{i}_dram", shape, _mybir.dt.float32, kind="ExternalOutput").ap())
    build(nc, ins, outs)
    r = _run(nc, [arrays], core_ids=[0])
    return tuple(r.results[0][f"out_{i}_dram"] for i in range(len(_OUTS)))
```
